# Optimizing a Trainium2 kernel written in Bass

```python
import math
import jax, jax.numpy as jnp
from jax import lax
import numpy as np

D_MODEL = 2048
BATCH = 1
SEQ = 256
DEPTH = 1

PLE_DIM = 256
D_MIX = D_MODEL
MLSTM_HEADS = 4
MLSTM_HEAD_DIM = (D_MIX // 2) // MLSTM_HEADS
MLSTM_WIDTH = MLSTM_HEADS * MLSTM_HEAD_DIM
MLSTM_CHUNK = 64
FOX_HEADS = 8
FOX_HEAD_DIM = (D_MIX - MLSTM_WIDTH) // FOX_HEADS
FOX_WIDTH = FOX_HEADS * FOX_HEAD_DIM
FOX_BLOCK = 128
D_FF = ((8 * D_MODEL // 3 + 255) // 256) * 256
CONV_WIDTH = 3
EPS = 1e-6
IN_SIZES = (MLSTM_WIDTH, MLSTM_WIDTH, MLSTM_WIDTH, MLSTM_WIDTH, MLSTM_HEADS, MLSTM_HEADS,
            FOX_WIDTH, FOX_WIDTH, FOX_WIDTH, FOX_HEADS)
IN_TOTAL = sum(IN_SIZES)


def rms_norm(x, g):
    xf = x.astype(jnp.float32)
    y = xf * lax.rsqrt(jnp.mean(xf * xf, axis=-1, keepdims=True) + EPS)
    return (y * g.astype(jnp.float32)).astype(x.dtype)

def mlstm_chunkwise(q, k, v, ig, lf):
    B, H, S, d = q.shape
    L = MLSTM_CHUNK
    nc = S // L
    k = k * (d ** -0.5)

    def to_chunks(t):
        return jnp.moveaxis(t.reshape((B, H, nc, L) + t.shape[3:]), 2, 0)

    qc, kc, vc = to_chunks(q), to_chunks(k), to_chunks(v)
    igc = to_chunks(ig)
    bc = jnp.cumsum(to_chunks(lf), axis=-1)
    causal = jnp.tril(jnp.ones((L, L), dtype=bool))

    def step(carry, inp):
        C, n, m = carry
        qi, ki, vi, ii, bi = inp
        inter = bi + m[..., None]
        D = jnp.where(causal, bi[..., :, None] - bi[..., None, :] + ii[..., None, :], -jnp.inf)
        m_comb = jnp.maximum(inter, jnp.max(D, axis=-1))
        w_intra = jnp.exp(D - m_comb[..., None])
        w_inter = jnp.exp(inter - m_comb)
        s = jnp.einsum('bhtd,bhsd->bhts', qi, ki) * w_intra
        num = jnp.einsum('bhts,bhsv->bhtv', s, vi) + w_inter[..., None] * jnp.einsum('bhtk,bhkv->bhtv', qi, C)
        den = jnp.sum(s, axis=-1) + w_inter * jnp.einsum('bhtk,bhk->bht', qi, n)
        h = num / jnp.maximum(jnp.abs(den), jnp.exp(-m_comb))[..., None]
        bL = bi[..., -1]
        g = bL[..., None] - bi + ii
        m_new = jnp.maximum(bL + m, jnp.max(g, axis=-1))
        wk = jnp.exp(g - m_new[..., None])
        decay = jnp.exp(bL + m - m_new)
        C = decay[..., None, None] * C + jnp.einsum('bhsk,bhsv->bhkv', ki * wk[..., None], vi)
        n = decay[..., None] * n + jnp.einsum('bhs,bhsk->bhk', wk, ki)
        return (C, n, m_new), h

    init = (jnp.zeros((B, H, d, d), jnp.float32), jnp.zeros((B, H, d), jnp.float32),
            jnp.zeros((B, H), jnp.float32))
    _, hs = lax.scan(step, init, (qc, kc, vc, igc, bc))
    return jnp.moveaxis(hs, 0, 2).reshape(B, H, S, d)

def forgetting_attention(q, k, v, logf):
    B, S, H, d = q.shape
    nb = S // FOX_BLOCK
    F = jnp.cumsum(logf, axis=1).transpose(0, 2, 1)
    kt = k.transpose(0, 2, 1, 3)
    vt = v.transpose(0, 2, 1, 3)
    qb = q.reshape(B, nb, FOX_BLOCK, H, d).transpose(1, 0, 3, 2, 4)
    Fq = F.reshape(B, H, nb, FOX_BLOCK).transpose(2, 0, 1, 3)
    kpos = jnp.arange(S)
    scale = d ** -0.5

    def one_block(args):
        qi, Fqi, bi = args
        qpos = bi * FOX_BLOCK + jnp.arange(FOX_BLOCK)
        s = jnp.einsum('bhqd,bhkd->bhqk', qi, kt, preferred_element_type=jnp.float32) * scale
        s = s + Fqi[..., None] - F[:, :, None, :]
        s = jnp.where(kpos[None, :] <= qpos[:, None], s, -jnp.inf)
        pr = jax.nn.softmax(s, axis=-1)
        return jnp.einsum('bhqk,bhkd->bhqd', pr.astype(vt.dtype), vt)

    out = lax.map(one_block, (qb, Fq, jnp.arange(nb)))
    return out.transpose(1, 0, 3, 2, 4).reshape(B, S, H * d)

def causal_dwconv(a, w, b):
    y = lax.conv_general_dilated(a, w[:, None, :].astype(a.dtype), window_strides=(1,),
                                 padding=[(CONV_WIDTH - 1, 0)],
                                 dimension_numbers=('NWC', 'WIO', 'NWC'),
                                 feature_group_count=a.shape[-1])
    return y + b.astype(a.dtype)

def first_inputs(seed: int = 0) -> dict:
    key = jax.random.key(seed)
    ks = jax.random.split(key, 20)
    nrm = jax.random.normal
    f32 = jnp.float32
    x = nrm(ks[0], (BATCH, SEQ, D_MODEL), f32)
    p = nrm(ks[1], (DEPTH, BATCH, SEQ, PLE_DIM), f32)
    mix_norm_g = 1.0 + 0.02 * nrm(ks[2], (DEPTH, D_MODEL), f32)
    w_in = nrm(ks[3], (DEPTH, D_MODEL, IN_TOTAL), f32) * D_MODEL ** -0.5
    m_i_bias = 0.1 * nrm(ks[4], (DEPTH, MLSTM_HEADS), f32)
    m_f_bias = jnp.linspace(3.0, 6.0, MLSTM_HEADS, dtype=f32)[None, :] + 0.01 * nrm(ks[5], (DEPTH, MLSTM_HEADS), f32)
    mlstm_gate_bias = jnp.concatenate([m_i_bias, m_f_bias], axis=-1)
    mlstm_out_g = 1.0 + 0.02 * nrm(ks[6], (DEPTH, MLSTM_WIDTH), f32)
    fox_q_g = 1.0 + 0.02 * nrm(ks[7], (DEPTH, FOX_HEAD_DIM), f32)
    fox_k_g = 1.0 + 0.02 * nrm(ks[8], (DEPTH, FOX_HEAD_DIM), f32)
    fox_f_bias = jnp.linspace(1.0, 5.0, FOX_HEADS, dtype=f32)[None, :] + 0.01 * nrm(ks[9], (DEPTH, FOX_HEADS), f32)
    w_out = nrm(ks[10], (DEPTH, D_MIX, D_MODEL), f32) * D_MIX ** -0.5
    ffn_norm_g = 1.0 + 0.02 * nrm(ks[11], (DEPTH, D_MODEL), f32)
    w_up = nrm(ks[12], (DEPTH, D_MODEL, 2 * D_FF), f32) * D_MODEL ** -0.5
    conv_w = nrm(ks[13], (DEPTH, CONV_WIDTH, D_FF), f32) * CONV_WIDTH ** -0.5
    conv_b = 0.02 * nrm(ks[14], (DEPTH, D_FF), f32)
    w_down = nrm(ks[15], (DEPTH, D_FF, D_MODEL), f32) * D_FF ** -0.5
    ple_norm_g = 1.0 + 0.02 * nrm(ks[16], (DEPTH, D_MODEL), f32)
    w_ple_gate = nrm(ks[17], (DEPTH, D_MODEL, D_MODEL), f32) * D_MODEL ** -0.5
    w_ple_proj = nrm(ks[18], (DEPTH, PLE_DIM, D_MODEL), f32) * PLE_DIM ** -0.5
    return {"x": x, "p": p, "mix_norm_g": mix_norm_g, "w_in": w_in,
            "mlstm_gate_bias": mlstm_gate_bias, "mlstm_out_g": mlstm_out_g,
            "fox_q_g": fox_q_g, "fox_k_g": fox_k_g, "fox_f_bias": fox_f_bias,
            "w_out": w_out, "ffn_norm_g": ffn_norm_g, "w_up": w_up, "conv_w": conv_w,
            "conv_b": conv_b, "w_down": w_down, "ple_norm_g": ple_norm_g,
            "w_ple_gate": w_ple_gate, "w_ple_proj": w_ple_proj}

def first_block(x, p, mix_norm_g, w_in, mlstm_gate_bias, mlstm_out_g, fox_q_g, fox_k_g, fox_f_bias,
              w_out, ffn_norm_g, w_up, conv_w, conv_b, w_down, ple_norm_g, w_ple_gate, w_ple_proj):
    B, S, _ = x.shape
    f32 = jnp.float32
    split_points = np.cumsum(IN_SIZES)[:-1].tolist()
    for i in range(DEPTH):
        h = rms_norm(x, mix_norm_g[i])
        z = h @ w_in[i]
        mq, mk, mv, mo, mi, mf, fq, fk, fv, ff = jnp.split(z, split_points, axis=-1)

        def heads_a(t):
            return t.reshape(B, S, MLSTM_HEADS, MLSTM_HEAD_DIM).transpose(0, 2, 1, 3).astype(f32)
        ig = (mi + mlstm_gate_bias[i, :MLSTM_HEADS]).astype(f32).transpose(0, 2, 1)
        lf = jax.nn.log_sigmoid((mf + mlstm_gate_bias[i, MLSTM_HEADS:]).astype(f32)).transpose(0, 2, 1)
        ha = mlstm_chunkwise(heads_a(mq), heads_a(mk), heads_a(mv), ig, lf)
        ha = rms_norm(ha.transpose(0, 2, 1, 3), mlstm_out_g[i].reshape(MLSTM_HEADS, MLSTM_HEAD_DIM))
        ha = (ha.reshape(B, S, MLSTM_WIDTH) * jax.nn.sigmoid(mo.astype(f32))).astype(x.dtype)

        qb = rms_norm(fq.reshape(B, S, FOX_HEADS, FOX_HEAD_DIM), fox_q_g[i])
        kb = rms_norm(fk.reshape(B, S, FOX_HEADS, FOX_HEAD_DIM), fox_k_g[i])
        vb = fv.reshape(B, S, FOX_HEADS, FOX_HEAD_DIM)
        logf = jax.nn.log_sigmoid((ff + fox_f_bias[i]).astype(f32))
        hb = forgetting_attention(qb, kb, vb, logf).astype(x.dtype)

        x = x + jnp.concatenate([ha, hb], axis=-1) @ w_out[i]

        h = rms_norm(x, ffn_norm_g[i])
        u = h @ w_up[i]
        a, g = jnp.split(u, 2, axis=-1)
        a = causal_dwconv(a, conv_w[i], conv_b[i])
        x = x + (jax.nn.gelu(a, approximate=False) * g) @ w_down[i]

        gate = jax.nn.sigmoid(rms_norm(x, ple_norm_g[i]) @ w_ple_gate[i])
        x = x + gate * (p[i].astype(x.dtype) @ w_ple_proj[i])
    return x


D_MIX_2 = D_MODEL
CONV_W = D_MIX_2 // 2
CONV_GROUPS = 16
GLA_HEADS = 4
GLA_DV = D_MIX_2 - CONV_W
HEAD_V = GLA_DV // GLA_HEADS
GLA_DK = GLA_DV // 2
HEAD_K = GLA_DK // GLA_HEADS
GATE_RANK = 16
GATE_TAU = 16
CHUNK = 64
CONV_K = 3
D_FF_2 = 5632
D_IN = 3 * CONV_W + 2 * GLA_DK + 2 * GLA_DV + GATE_RANK


def rmsnorm(x, w):
    x32 = x.astype(jnp.float32)
    y = x32 * lax.rsqrt(jnp.mean(x32 * x32, axis=-1, keepdims=True) + EPS)
    return (y * w.astype(jnp.float32)).astype(x.dtype)

def causal_dwconv3(u, w):
    s = u.shape[1]
    up = jnp.pad(u, ((0, 0), (CONV_K - 1, 0), (0, 0)))
    return up[:, :s] * w[0] + up[:, 1:s + 1] * w[1] + up[:, 2:] * w[2]

def gla_chunked(q, k, v, log_a):
    bsz, s, h, dk = q.shape
    dv = v.shape[-1]
    nc = s // CHUNK

    def to_chunks(t):
        return t.reshape(bsz, nc, CHUNK, h, t.shape[-1]).transpose(1, 0, 3, 2, 4).astype(jnp.float32)

    mask = jnp.tril(jnp.ones((CHUNK, CHUNK), dtype=bool))[None, None, :, :, None]

    def step(state, inp):
        qc, kc, vc, gc = inp
        b = jnp.cumsum(gc, axis=2)
        diff = b[:, :, :, None, :] - b[:, :, None, :, :]
        decay = jnp.exp(jnp.where(mask, diff, -jnp.inf))
        scores = jnp.einsum('bhid,bhjd,bhijd->bhij', qc, kc, decay)
        o = jnp.einsum('bhij,bhje->bhie', scores, vc) + jnp.einsum('bhid,bhde->bhie', qc * jnp.exp(b), state)
        b_last = b[:, :, -1:, :]
        state = jnp.exp(b_last[:, :, 0, :])[..., None] * state + jnp.einsum(
            'bhjd,bhje->bhde', kc * jnp.exp(b_last - b), vc)
        return state, o

    state0 = jnp.zeros((bsz, h, dk, dv), jnp.float32)
    _, o = lax.scan(step, state0, (to_chunks(q), to_chunks(k), to_chunks(v), to_chunks(log_a)))
    return o.transpose(1, 0, 3, 2, 4).reshape(bsz, s, h, dv)

def hybrid_mixer(h, w_in, conv_w, gate_w2, gate_b, gla_norm_w, w_out):
    bsz, s, _ = h.shape
    proj = h @ w_in
    splits = np.cumsum([CONV_W, CONV_W, CONV_W, GLA_DK, GLA_DK, GLA_DV, GLA_DV])
    cb, cc, cx, q, k, v, r, a_lr = jnp.split(proj, splits, axis=-1)
    y_conv = cb * causal_dwconv3(cc * cx, conv_w)
    log_a = jax.nn.log_sigmoid((a_lr @ gate_w2 + gate_b).astype(jnp.float32)) / GATE_TAU
    q = q.reshape(bsz, s, GLA_HEADS, HEAD_K) * (HEAD_K ** -0.5)
    k = k.reshape(bsz, s, GLA_HEADS, HEAD_K)
    v = v.reshape(bsz, s, GLA_HEADS, HEAD_V)
    log_a = log_a.reshape(bsz, s, GLA_HEADS, HEAD_K)
    o = gla_chunked(q, k, v, log_a).astype(h.dtype)
    o = rmsnorm(o, gla_norm_w) * jax.nn.silu(r.reshape(bsz, s, GLA_HEADS, HEAD_V))
    y_gla = o.reshape(bsz, s, GLA_DV)
    return jnp.concatenate([y_conv, y_gla], axis=-1) @ w_out

def conv_ffn(h, w_up, ffn_conv_w, w_down):
    u = causal_dwconv3(h @ w_up, ffn_conv_w)
    g, val = jnp.split(u, 2, axis=-1)
    return (jax.nn.silu(g) * val) @ w_down

def second_inputs(seed: int = 0) -> dict:
    key = jax.random.key(seed)
    ks = jax.random.split(key, 20)
    n = jax.random.normal
    f = jnp.float32
    L = DEPTH
    return {
        "x": n(ks[0], (BATCH, SEQ, D_MODEL), f),
        "c": n(ks[1], (BATCH, D_MODEL), f),
        "w_mod": n(ks[2], (L, D_MODEL, 6 * D_MODEL), f) * (0.5 * D_MODEL ** -0.5),
        "b_mod": 0.01 * n(ks[3], (L, 6 * D_MODEL), f),
        "mix_pre_w": 1.0 + 0.05 * n(ks[4], (L, D_MODEL), f),
        "mix_post_w": 1.0 + 0.05 * n(ks[5], (L, D_MODEL), f),
        "w_in": n(ks[6], (L, D_MODEL, D_IN), f) * D_MODEL ** -0.5,
        "conv_w": n(ks[7], (L, CONV_K, CONV_W), f) * CONV_K ** -0.5,
        "gate_w2": n(ks[8], (L, GATE_RANK, GLA_DK), f) * GATE_RANK ** -0.5,
        "gate_b": 0.01 * n(ks[9], (L, GLA_DK), f),
        "gla_norm_w": 1.0 + 0.05 * n(ks[10], (L, HEAD_V), f),
        "w_out": n(ks[11], (L, D_MIX_2, D_MODEL), f) * D_MIX_2 ** -0.5,
        "ffn_pre_w": 1.0 + 0.05 * n(ks[12], (L, D_MODEL), f),
        "ffn_post_w": 1.0 + 0.05 * n(ks[13], (L, D_MODEL), f),
        "w_up": n(ks[14], (L, D_MODEL, 2 * D_FF_2), f) * D_MODEL ** -0.5,
        "ffn_conv_w": n(ks[15], (L, CONV_K, 2 * D_FF_2), f) * CONV_K ** -0.5,
        "w_down": n(ks[16], (L, D_FF_2, D_MODEL), f) * D_FF_2 ** -0.5,
    }

def second_block(x, c, w_mod, b_mod, mix_pre_w, mix_post_w, w_in, conv_w, gate_w2, gate_b, gla_norm_w,
              w_out, ffn_pre_w, ffn_post_w, w_up, ffn_conv_w, w_down):
    c_act = jax.nn.silu(c)
    for l in range(DEPTH):
        mod = (c_act @ w_mod[l] + b_mod[l])[:, None, :]
        sh_m, sc_m, g_m, sh_f, sc_f, g_f = jnp.split(mod, 6, axis=-1)
        h = rmsnorm(x, mix_pre_w[l]) * (1 + sc_m) + sh_m
        y = hybrid_mixer(h, w_in[l], conv_w[l], gate_w2[l], gate_b[l], gla_norm_w[l], w_out[l])
        x = x + g_m * rmsnorm(y, mix_post_w[l])
        h = rmsnorm(x, ffn_pre_w[l]) * (1 + sc_f) + sh_f
        y = conv_ffn(h, w_up[l], ffn_conv_w[l], w_down[l])
        x = x + g_f * rmsnorm(y, ffn_post_w[l])
    return x


def setup_inputs(seed=0):
    out = dict(first_inputs(seed))
    for name, value in second_inputs(seed + 1).items():
        if name != "x":
            out[name + "_2"] = value
    return out


def reference(
    x, p, mix_norm_g, w_in, mlstm_gate_bias, mlstm_out_g, fox_q_g, fox_k_g, fox_f_bias, w_out,
    ffn_norm_g, w_up, conv_w, conv_b, w_down, ple_norm_g, w_ple_gate, w_ple_proj, c_2, w_mod_2,
    b_mod_2, mix_pre_w_2, mix_post_w_2, w_in_2, conv_w_2, gate_w2_2, gate_b_2, gla_norm_w_2,
    w_out_2, ffn_pre_w_2, ffn_post_w_2, w_up_2, ffn_conv_w_2, w_down_2,
):
    x = first_block(
        x, p, mix_norm_g, w_in, mlstm_gate_bias, mlstm_out_g, fox_q_g, fox_k_g, fox_f_bias,
        w_out, ffn_norm_g, w_up, conv_w, conv_b, w_down, ple_norm_g, w_ple_gate, w_ple_proj,
    )
    return second_block(
        x, c_2, w_mod_2, b_mod_2, mix_pre_w_2, mix_post_w_2, w_in_2, conv_w_2, gate_w2_2,
        gate_b_2, gla_norm_w_2, w_out_2, ffn_pre_w_2, ffn_post_w_2, w_up_2, ffn_conv_w_2,
        w_down_2,
    )


_drawn_inputs = setup_inputs


def setup_inputs(seed=0):
    import zlib

    import numpy as np

    out = dict(_drawn_inputs(seed))
    spreads = {}
    factors = {'mlstm_out_g': 7.127,
     'fox_q_g': 8.0,
     'fox_k_g': 8.0,
     'ffn_norm_g': 3.949,
     'conv_b': 5.588,
     'ple_norm_g': 200.0,
     'b_mod_2': 4.752,
     'mix_pre_w_2': 12.787,
     'mix_post_w_2': 42.672,
     'gate_w2_2': 3.214,
     'gate_b_2': 200.0,
     'gla_norm_w_2': 200.0,
     'ffn_pre_w_2': 19.517,
     'ffn_post_w_2': 43.632}
    for name, (base, spread) in spreads.items():
        noise = np.random.default_rng([zlib.crc32(name.encode()), seed]).standard_normal(out[name].shape)
        drawn = base * np.exp(spread * noise) if base else spread * noise
        out[name] = __import__('jax').numpy.asarray(drawn.astype(out[name].dtype))
    for name, factor in factors.items():
        out[name] = (out[name] * factor).astype(out[name].dtype)
    return out
```

```python
from concourse import bass, mybir

F32 = mybir.dt.float32
F32R = mybir.dt.float32r
I32 = mybir.dt.int32
ALU = mybir.AluOpType
ACT = mybir.ActivationFunctionType
AX_X = mybir.AxisListType.X

P = 128
T = 256
D = 2048
KC = D // P
EPS = 1e-6
STRIP = 512
NB = STRIP // P
GK = 2
RING = 4

MH, MD = 4, 256
FH, FD = 8, 128
GH, GDK, GDV = 4, 128, 256
GATE_TAU = 16.0
D_FF = 5632
FB = D_FF // P
FOX_OUT = MH * MD // P
N_MOD = 6 * D // STRIP
MOD_RING = 4
NORM_CHUNKS = (2, 2, 4, 4, 4)
NEG = -1.0e30

PARAM_ROWS = [
    ("mix_norm_g", KC), ("ffn_norm_g", KC), ("ple_norm_g", KC), ("mlstm_out_g", 8), ("fox_q_g", 1), ("fox_k_g", 1),
    ("c_2", KC), ("mix_pre_w_2", KC), ("mix_post_w_2", KC), ("ffn_pre_w_2", KC), ("ffn_post_w_2", KC),
    ("gate_b_2", 4), ("gla_norm_w_2", 2), ("conv_w_2", 24), ("b_mod_2", 96),
    ("conv_w", 3 * FB), ("conv_b", FB), ("ffn_conv_w_2", 6 * FB),
]
PCOL = {}
N_PAR = 0
for _name, _rows in PARAM_ROWS:
    PCOL[_name] = N_PAR
    N_PAR += _rows
PAR_TILES = -(-N_PAR // P)


def par_pieces():
    pieces = []
    for name, rows in PARAM_ROWS:
        done = 0
        while done < rows:
            r = PCOL[name] + done
            n = min(rows - done, P - r % P)
            pieces.append((name, done, n, r % P, r // P))
            done += n
    return pieces


class Layer:
    count_g = 0
    count_n = 0
    count_h = 0

    def __init__(self, pairs, groups, unrolled=False, mod=None, mod_per_pair=1, mod_first=0, mod_pairs=None, residual=False,
                 joined=False):
        self.pairs, self.G, self.unrolled, self.residual = pairs, groups, unrolled, residual
        self.joined = joined
        self.mod, self.mod_per_pair, self.mod_first = mod, mod_per_pair, mod_first
        self.mod_pairs = pairs if mod_pairs is None else mod_pairs
        self.g0, self.n0, self.h0 = Layer.count_g, Layer.count_n, Layer.count_h
        Layer.count_g += 2 * pairs * groups
        Layer.count_n += 2 * pairs
        Layer.count_h += 0 if residual else 2 * pairs - int(joined)

    def group(self, i, s, j):
        return i * (2 * self.G) + (self.g0 + s * self.G + j)

    def slot(self, s, j):
        return (self.g0 + s * self.G + j) % RING

    def slot_int(self, i, s, j):
        return (self.g0 + (2 * i + s) * self.G + j) % RING

    def strip(self, i, s):
        return i * 2 + (self.n0 + s)

    def halved(self, i, s):
        return i * 2 + (self.h0 + s + 1)

    def joins(self, i, s):
        return self.joined and (i, s) == (self.pairs - 1, 1)

    def takes_mod(self, i):
        return self.mod is not None and (self.mod_pairs == self.pairs or i < self.mod_pairs)

    @property
    def end(self):
        return self.n0 + 2 * self.pairs

    @property
    def end_g(self):
        return self.g0 + 2 * self.pairs * self.G


def plan_layers():
    Layer.count_g = Layer.count_n = Layer.count_h = 0
    g16, g44 = KC // GK, FB // GK
    return {
        "in1a": Layer(1, g16, unrolled=True), "in1b": Layer(6, g16, unrolled=True, mod=0, mod_pairs=3),
        "out1": Layer(2, g16, unrolled=True, residual=True, joined=True),
        "up1": Layer(11, g16, mod=3), "down1": Layer(2, g44, unrolled=True, mod=14, mod_per_pair=2, residual=True, joined=True),
        "gate1a": Layer(1, g16, unrolled=True, mod=18), "proj": Layer(2, 1, unrolled=True),
        "gate1b": Layer(1, g16, unrolled=True, joined=True),
        "in2": Layer(6, g16, unrolled=True, mod=19, mod_pairs=1), "out2": Layer(2, g16, unrolled=True, joined=True),
        "up2": Layer(11, g16), "down2": Layer(2, g44, unrolled=True, mod=20, mod_per_pair=2, joined=True),
    }


class Steps:

    def __init__(self, eng, sem):
        self.eng, self.sem, self.n, self.i, self.per = eng, sem, 0, None, 0

    def mark(self, ins):
        ins.then_inc(self.sem, 1)
        self.n += 1

    def wait(self):
        self.eng.wait_ge(self.sem, self.n if self.i is None else self.i * self.per + (self.n - self.first * self.per))

    def do(self, ins):
        self.mark(ins)
        self.wait()

    def enter(self, i, per, first=0):
        self.i, self.per, self.first, self.start = i, per, first, self.n

    def leave(self, times):
        assert self.n - self.start == self.per, (self.n - self.start, self.per)
        self.n, self.i = self.start + self.per * times, None


class Tally(dict):

    def next(self, name, by=1):
        self[name] = self.get(name, 0) + by
        return self[name]


def for_pairs(eng, layer, body, steps=None, per=0, peel=False):
    if layer.unrolled:
        for i in range(layer.pairs):
            body(i)
        return
    if peel:
        body(0, True)
    with eng.Fori(int(peel), layer.pairs) as i:
        if steps:
            steps.enter(i, per, int(peel))
        body(i)
        if steps:
            steps.leave(layer.pairs - int(peel))


def two_block_kernel(nc, a, out):
    layers = plan_layers()
    g16 = KC // GK
    total_groups = max(l.end_g for l in layers.values())

    def blocks(ap):
        return ap.rearrange("(c p) n -> p c n", p=P)

    w_in1, w_out1, w_up1, w_down1 = (blocks(a[k][0]) for k in ("w_in", "w_out", "w_up", "w_down"))
    w_gate1, w_proj1 = blocks(a["w_ple_gate"][0]), blocks(a["w_ple_proj"][0])
    w_mod = blocks(a["w_mod_2"][0])
    w_in2, w_out2, w_up2, w_down2 = (blocks(a[k][0]) for k in ("w_in_2", "w_out_2", "w_up_2", "w_down_2"))
    M_GATES = 4 * D // 2
    FOX0 = M_GATES + 2 * MH
    F_GATES = FOX0 + 3 * D // 2
    A_LR = 6144

    def plain(w, first=0):
        return lambda i, s, j: w[:, GK * j:GK * j + GK, ((2 * i + s) + first) * STRIP:((2 * i + s) + first + 1) * STRIP]

    def up(w):
        return lambda i, s, j: w[:, GK * j:GK * j + GK, bass.ds(i * STRIP + s * D_FF, STRIP)]

    in1_strips = [(FOX0 + e * 1024 + f * STRIP, 32 + e * 8 + f * NB) for f in range(2) for e in range(3)] \
        + [(e * 1024 + f * STRIP, e * 8 + f * NB) for f in range(2) for e in range(3)] \
        + [(3 * 1024 + f * STRIP, 24 + f * NB) for f in range(2)]

    in2_strips = [(3072, 24), (3584, 28), (4096, 32), (4608, 36), (1024, 8), (2048, 16), (1536, 12), (2560, 20),
                  (0, 0), (512, 4), (5120, 40), (5632, 44)]

    def listed(w, strips):
        return lambda i, s, j: w[:, GK * j:GK * j + GK, strips[2 * i + s][0]:strips[2 * i + s][0] + STRIP]

    def rotated(w, first):
        return lambda i, s, j: w[:, (GK * j + first) % KC:(GK * j + first) % KC + GK,
                                 (2 * i + s) * STRIP:(2 * i + s + 1) * STRIP]

    source = {
        "in1a": listed(w_in1, in1_strips), "in1b": listed(w_in1, in1_strips[2:]), "out1": rotated(w_out1, FOX_OUT),
        "up1": up(w_up1),
        "down1": plain(w_down1), "gate1a": plain(w_gate1), "proj": plain(w_proj1), "gate1b": plain(w_gate1, 2),
        "in2": listed(w_in2, in2_strips),
        "out2": plain(w_out2), "up2": up(w_up2), "down2": plain(w_down2),
    }

    at = [-(-nc.sbuf_base // 32) * 32]
    place = {}

    def sb(name, shape, dt=F32, over=None, skip=0):
        size = 4
        for n in shape[1:]:
            size *= n
        if over is None:
            offset = at[0]
            at[0] += -(-size // 32) * 32
        else:
            offset = place[over] + skip
        place[name] = offset
        return nc.alloc_sbuf_tensor_at(name, shape, dt, offset=offset)

    w_raw = sb("w_raw", [P, RING, GK, STRIP])
    w_hi = sb("w_hi", [P, RING, GK, STRIP], F32R)
    w_lo = sb("w_lo", [P, RING, GK, STRIP], F32R)
    xs = sb("xs", [P, KC, 2 * T], F32R)
    y2 = sb("y2", [P, KC, T], over="xs")
    xT = sb("xT", [P, KC, T])
    hs = sb("hs", [P, FB, 2 * T], F32R)
    mix = sb("mix", [P, 2 * FB, T], over="hs")
    g_hi = sb("g_hi", [P, KC, P], F32R, over="hs", skip=72 * T * 4)
    g_lo = sb("g_lo", [P, KC, P], F32R, over="hs", skip=80 * T * 4)
    ps_in = sb("ps_in", [P, GK, 2 * T], F32R, over="hs", skip=72 * T * 4)
    xf = sb("xf", [P, FH, 2 * T], F32R, over="hs", skip=40 * T * 4)
    cf = [sb(f"cf{k}", [P, NB, 2 * T], F32R, over="hs", skip=blk * T * 4)
          for k, blk in enumerate((8, 60))]
    par = sb("par", [P, N_PAR])
    modT = sb("modT", [P, 6 * KC])
    mod_acc = sb("mod_acc", [P, STRIP])
    mod_w = sb("mod_w", [P, MOD_RING, STRIP])
    conv_tmp = sb("conv_tmp", [P, NB, T], over="mod_w")
    ident = sb("ident", [P, P])
    ones = sb("ones", [P, P])
    causal = sb("causal", [P, P])
    causalT = sb("causalT", [P, P])
    ssum = sb("ssum", [P, T], over="causal")
    half = sb("half", [P, NB, T])
    act_out = sb("act_out", [P, NB, T])
    conv_p = sb("conv_p", [P, 4, NB])
    c_act = sb("c_act", [P, KC])
    gbias = sb("gbias", [P, 1])
    table_of = sb("table_of", [P, 1])
    fox_qk_g = sb("fox_qk_g", [P, 1])

    PS = nc.alloc_psum_tensor("PS", [P, 8, STRIP], F32)

    def mixcols(blk, n):
        return mix[:, :, :].rearrange("p b t -> p (b t)")[:, blk * T:blk * T + n]

    x_rows = mixcols(16, 2 * D).rearrange("p (t d) -> p t d", t=2)
    y_rows = mixcols(40, 2 * D).rearrange("p (t d) -> p t d", t=2)
    par_rows = mixcols(38, PAR_TILES * P).rearrange("p (k d) -> p k d", d=P)
    g_raw = mixcols(60, KC * P).rearrange("p (c n) -> p c n", n=P)
    onehot = mixcols(68, FH * P).rearrange("p (h n) -> p h n", n=P)
    gate_w2 = mixcols(68, GH * GDK)[0:16, :]
    masks = mixcols(56, 7 * P).rearrange("p (l n) -> p l n", n=P)

    def sem(name):
        return nc.alloc_semaphore(name)

    x_loaded = [sem(f"x_loaded{k}") for k in range(4)]
    w_full = [sem(f"w_full{i}") for i in range(RING)]
    hi_made = sem("hi_made")
    lo_made = sem("lo_made")
    w_used = sem("w_used")
    half_made = sem("half_made")
    evac_done = sem("evac_done")
    mod_full = [sem(f"mod_full{i}") for i in range(MOD_RING)]
    mod_used = sem("mod_used")
    mod_sum = sem("mod_sum")
    mod_read = sem("mod_read")
    names = """gain_loaded gain_turned gain_made par_loaded gate_loaded
        gate2_loaded p_loaded gw2_loaded consts cleared pad2_zeroed masks_made
        x_turned x_copied par_turned par_made cact_made sq_made strip_sq sq_folded ss_made ss_read y_scaled
        gain_f var_made std_made hn_made hn_hi x_ready
        gate_hi gate_lo gate_ps gate_half gate_sum gate_ln gates_ready v_turned v_copied y_hi
        m_arg m_masked m_exp m_weighed m_num m_floor m_h m_sq m_ss m_var m_std m_og m_y
        f_sq f_ss f_var f_std f_rstd f_rows f_rows_copied f_spread f_normed cols_turned cols_made
        f_logits f_max f_exp f_probs f_turned f_copied f_out f_ready
        gelu_made h2_made h2_hi sig_made p_turned p_hi p_ready
        c_y r_silu g_lr g_pre g_ln g_arg g_decay g_qk g_score g_merged g_out g_sq g_o g_ss g_var g_std g_y
        embedded mixed res_made gs_made y_turned y_copied stored dve_step act_step""".split()
    S = {n: sem(n) for n in names}

    FOX_SUMS = {0: 0, 3: 1}
    FOX_NORM = {1: 0, 4: 1}
    FOX_PAIR = {2: 0, 3: 1, 5: 2, 6: 3}
    MLSTM = {7: 0, 8: 1, 10: 2, 11: 3}
    MLSTM_NORM = {8: 0, 9: 1, 11: 2}
    V_TURN = {2: 48, 5: 52, 7: 16, 10: 20}

    GLA_DECAY = {2: 0, 4: 1, 6: 2, 8: 3}
    GLA_HEAD = {3: 0, 5: 1, 7: 2, 9: 3}
    GLA_NORM = {4: 0, 6: 1, 8: 2, 10: 3}
    GLA_TURN = {3: 32, 5: 36}
    CONV_HALF = {7: 0, 9: 1}

    def spare(name, n):
        return 4 * ((layers[name].n0 + n + 1) % 2)

    def turned_values(blk):
        return mixcols(blk, 2 * STRIP).rearrange("p (t n) -> p t n", t=2)

    in1_rstd = mix[:, 67, :]
    ple_gate, ple_in = mix[:, 16:32, :], mix[:, 40:56, :]
    mixed = mix[:, 16:32, :]
    fox_sq = mix[:, 56:64, :]
    fox_rows = mix[0:2 * NB, 66, :]
    fox_rstd = mixcols(65, 4 * NB)
    m_sq, m_e, m_sd = mix[:, 56:58, :], mix[:, 60, :], mix[:, 62, :]
    m_w, m_sw = (act_out[:, 2 * k:2 * k + 2, :].rearrange("p a b -> p (a b)")[:, 0:3 * P] for k in range(2))
    m_u, m_negM, m_negFM, f_F, f_negF = (mix[0:n, b, :] for n, b in
                                         ((MH, 77), (MH, 79), (MH, 80), (FH, 81), (FH, 82)))

    gate_cols = mixcols(64, 64)[:, 32:32 + 2 * (FH + MH)]

    def f_col(t, h):
        return gate_cols[:, t * FH + h:t * FH + h + 1]

    def u_col(s, h):
        return gate_cols[:, 2 * FH + s * MH + h:2 * FH + s * MH + h + 1]

    def fox_l(h):
        return mixcols(72 + 2 * (h % 2), 3 * P)

    def fox_lT(h):
        return mixcols(83 + 2 * (h % 2), 3 * P)

    def fox_stat(h):
        return mixcols(64, 16)[:, 8 * (h % 2):8 * (h % 2) + 8]

    g_sq, g_sd, g_one = mix[:, 76:78, :], mix[:, 78, :], mix[:, 84, :]
    g_cum = mix[:, 72:76, :]
    g_qk = mix[:, 60:68, :]
    g_sc = mixcols(85, 3 * P)

    def halves(v, H):
        return v.rearrange("p (b e r) -> p b e r", e=2, r=H)

    def gla_place(l):
        return ((0, 0), (0, P), (1, 0), (1, T), (2, 0), (2, T), (3, 0), (3, T), (0, 0))[l]

    def x_turned(k):
        bank = 4 + 2 * (k % 2)
        return PS[:, bank:bank + 2, :].rearrange("p b (e t) -> p (b e) t", t=T)

    shift_m, scale_m, gate_m, shift_f, scale_f, gate_f = (modT[:, k * KC:(k + 1) * KC] for k in range(6))

    def mod_strip(layer, i, q):
        return i * layer.mod_per_pair + (layer.mod + q)

    def mod_tiles(layer, i, s, j):
        if not layer.takes_mod(i):
            return 0, range(0)
        if layer.mod_per_pair == 1:
            groups = 2 * layer.G - 4 - layer.mod_first
            return 0, range(*(min(KC, -(-max(0, k - layer.mod_first) * KC // groups)) for k in (s * layer.G + j, s * layer.G + j + 1)))
        first, groups = g16, layer.G - 4 - g16
        return s, range(*(min(KC, max(0, k - first) * KC // groups) for k in (j, j + 1)))

    def mod_sum_after(layer, i, s, j):
        if not layer.takes_mod(i):
            return None
        if layer.mod_per_pair == 1:
            return 0 if (s, j) == (1, layer.G - 2) else None
        return s if j == layer.G - 2 else None

    block = nc.Block()
    with block as block:

        @block.sync
        def _(sp):
            def load_params():
                for name, first, n, row, tile in par_pieces()[1:]:
                    src = a[name]
                    src = src.rearrange({2: "a b -> (a b)", 3: "a b c -> (a b c)"}[len(src.shape)]).rearrange("(r d) -> r d", d=P)
                    sp.dma_start(par_rows[row:row + n, tile, :], src[first:first + n, :]).then_inc(S["par_loaded"], 16)

            def stream(name):
                layer = layers[name]

                def pair(i):
                    for s in range(2):
                        for j in range(layer.G):
                            slot = layer.slot_int(i, s, j) if layer.unrolled else layer.slot(s, j)
                            if name == "in1a" and (i, s, j) == (0, 0, RING):
                                load_params()
                            sp.wait_ge(lo_made, layer.group(i, s, j) + 1)
                            sp.dma_start(w_raw[:, slot, :, :], source[name](i, s, j)).then_inc(w_full[slot], 16)

                for_pairs(sp, layer, pair)

            for k in range(4):
                cols = slice(k * STRIP, (k + 1) * STRIP)
                sp.dma_start(x_rows[:, :, cols], a["x"][0].rearrange("(t p) d -> p t d", p=P)[:, :, cols])\
                    .then_inc(x_loaded[k], 16)
            for name in layers:
                stream(name)
            for k in range(4):
                cols = slice(k * STRIP, (k + 1) * STRIP)
                sp.wait_ge(S["y_copied"], k + 1)
                sp.dma_start(out[0].rearrange("(t p) d -> p t d", p=P)[:, :, cols], y_rows[:, :, cols])\
                    .then_inc(S["stored"], 16)
            sp.wait_ge(S["stored"], 64)

        @block.gpsimd
        def _(pool):
            pool.sem_inc(lo_made, RING)
            pool.sem_inc(w_used, RING)
            pool.sem_inc(evac_done, 2)
            pool.sem_inc(mod_used, MOD_RING)
            pool.sem_inc(mod_read, 1)
            for tile, value in ((ident[:, :], 0.0), (ones[:, :], 1.0), (causal[:, :], 0.0), (causalT[:, :], 0.0),
                                (gbias[:, :], 0.0), (onehot[0:FH, :, :], 0.0), (g_raw, 0.0)):
                nc.gpsimd.memset(tile, value).then_inc(S["cleared"], 1)
            pool.wait_ge(S["cleared"], 7)
            for tile, op, fill, pattern, cm in (
                    (ident[:, :], ALU.not_equal, 1.0, [[-1, P]], 1),
                    (causal[:, :], ALU.is_ge, NEG, [[-1, P]], 1),
                    (causalT[:, :], ALU.is_ge, NEG, [[1, P]], -1),
                    (onehot[0:FH, :, :], ALU.not_equal, 1.0, [[-1, FH], [0, P]], 1)):
                nc.gpsimd.affine_select(out=tile, in_=tile, compare_op=op, fill=fill, base=0, pattern=pattern,
                                        channel_multiplier=cm).then_inc(S["consts"], 1)
            for dst, col, n in ((0, M_GATES, MH), (32, M_GATES + MH, MH), (64, F_GATES, FH)):
                pool.dma_start(g_raw[:, :, dst:dst + n], w_in1[:, :, col:col + n]).then_inc(S["gate_loaded"], 16)
            for dst, src in ((0, a["mlstm_gate_bias"][0, 0:MH]), (32, a["mlstm_gate_bias"][0, MH:2 * MH]),
                             (64, a["fox_f_bias"][0, :])):
                n = src.shape[0]
                pool.dma_start(gbias[dst:dst + n, :], src.rearrange("(p a) -> p a", a=1)).then_inc(S["gate_loaded"], 16)

            def mod_load(strip):
                for k in range(KC):
                    pool.wait_ge(mod_used, strip * KC + (k + 1))
                    pool.dma_start(mod_w[:, k % MOD_RING, :], w_mod[:, k, bass.ds(strip * STRIP, STRIP)])\
                        .then_inc(mod_full[k % MOD_RING], 16)

            with pool.Fori(0, layers["in2"].mod) as strip:
                mod_load(strip)
            pool.wait_ge(evac_done, 2 + layers["down1"].end)
            nc.gpsimd.memset(g_raw, 0.0).then_inc(S["pad2_zeroed"], 1)
            pool.wait_ge(S["pad2_zeroed"], 1)
            pool.dma_start(g_raw[:, :, 0:16], w_in2[:, :, A_LR:A_LR + 16]).then_inc(S["gate2_loaded"], 16)
            pool.dma_start(gate_w2, a["gate_w2_2"][0]).then_inc(S["gw2_loaded"], 16)
            nc.gpsimd.memset(masks, 1.0).then_inc(S["pad2_zeroed"], 1)
            pool.wait_ge(S["pad2_zeroed"], 2)
            for l in range(7):
                H = 64 >> l
                n = P // (2 * H)
                m = masks[:, l, :].rearrange("p (b e r) -> p b e r", e=2, r=H)
                for k, (pattern, base, cm) in enumerate((
                        ([[-2 * H, n], [0, 2], [0, H]], 0, 1),
                        ([[2 * H, n], [0, 2], [0, H]], H - 1, -1),
                        ([[0, n], [1, 2], [0, H]], -1, 0))):
                    nc.gpsimd.affine_select(out=m, in_=m, compare_op=ALU.is_ge, fill=0.0, base=base, pattern=pattern,
                                            channel_multiplier=cm).then_inc(S["masks_made"], 1)
                    pool.wait_ge(S["masks_made"], 3 * l + k + 1)
            with pool.Fori(layers["in2"].mod, layers["down2"].mod) as strip:
                mod_load(strip)
            pool.wait_ge(evac_done, 2 + layers["up2"].end)
            with pool.Fori(layers["down2"].mod, N_MOD) as strip:
                mod_load(strip)

        @block.scalar
        def _(act):
            steps = Steps(act, S["act_step"])
            tally = Tally()

            def wait(name, by=1):
                act.wait_ge(S[name], tally.next(name, by))

            def split_hi(layer, i, s, j):
                slot = layer.slot_int(i, s, j) if layer.unrolled else layer.slot(s, j)
                if isinstance(i, int):
                    g = layer.group(i, s, j) + RING
                    if g >= total_groups:
                        return
                    act.wait_ge(w_full[slot], 16 * (g // RING + 1))
                else:
                    act.wait_ge(w_full[slot], i * (16 * 2 * layer.G // RING) + 16 * ((layer.g0 + s * layer.G + j) // RING + 2))
                act.wait_ge(w_used, layer.group(i, s, j) + 1 + RING)
                nc.scalar.activation(w_hi[:, slot, :, :], w_raw[:, slot, :, :], ACT.Copy).then_inc(hi_made, 1)

            def copy_half(layer, i, s):
                n = layer.strip(i, s)
                act.wait_ge(w_used, layer.group(i, s, layer.G - 1) + 1 + RING)
                act.wait_ge(evac_done, n + 2)
                st = 4 * ((layer.n0 + s) % 2)
                nc.scalar.activation(half[:, :, :], PS[:, st:st + NB, T:2 * T], ACT.Copy).then_inc(half_made, 1)

            def stream(name, piece=None, side=None):
                layer = layers[name]

                def pair(i, first=False):
                    for s in range(2):
                        for j in range(layer.G):
                            if j == layer.G - 1 and not layer.residual and not layer.joins(i, s):
                                copy_half(layer, i, s)
                            split_hi(layer, i, s, j)
                            if piece and (s or not first):
                                piece(layer, i if s else i - 1, 1 - s, j)
                            if side:
                                side(2 * i + s, j)

                for_pairs(act, layer, pair, peel=piece is not None)

            def all_out(name):
                act.wait_ge(evac_done, 2 + layers[name].end)

            def squares(src, dst, made=None):
                for k in range(4):
                    if made:
                        wait(made)
                    nc.scalar.activation(dst[:, 4 * k:4 * k + 4, :], src[:, 4 * k:4 * k + 4, :], ACT.Square)\
                        .then_inc(S["sq_made"], 1)

            def strip_squares(src, k):
                if k:
                    wait("ss_read")
                nc.scalar.activation(act_out[:, :, :], src[:, NB * k:NB * k + NB, :], ACT.Square).then_inc(S["strip_sq"], 1)
                tally.next("strip_sq")

            def scale_strip(y, gain, k):
                act.wait_ge(S["strip_sq"], tally["strip_sq"])
                for c in range(NB * k, NB * k + NB):
                    ins = nc.scalar.activation(y[:, c, :], y[:, c, :], ACT.Copy, scale=gain[:, c:c + 1])
                ins.then_inc(S["y_scaled"], 1)

            def last_squares(name):
                layer = layers[name]
                act.wait_ge(w_used, RING + layer.end_g)
                wait("ss_read")
                nc.scalar.activation(act_out[:, :, :], PS[:, 4:8, 0:T], ACT.Square).then_inc(S["strip_sq"], 1)
                tally.next("strip_sq")

            def scale_last(y, gain):
                for b in range(NB):
                    c = 3 * NB + b
                    ins = nc.scalar.activation(y[:, c, :], PS[:, 4 + b, 0:T], ACT.Copy, scale=gain[:, c:c + 1])
                ins.then_inc(evac_done, 1)

            def preload(func):
                steps.wait()
                steps.mark(nc.scalar.activation(table_of[:, :], ones[:, 0:1], func))

            def squares_beside(name, src, gain=None, made=None):
                def side(n, j):
                    if n and j == 2:
                        act.wait_ge(evac_done, layers[name].n0 + n + 2)
                        strip_squares(src, n - 1)
                    if gain is not None and n and j == 3:
                        if made:
                            wait(made)
                        scale_strip(src, gain, n - 1)
                return side

            def std(var=mix[:, 36, :], sd=mix[:, 37, :]):
                wait("var_made")
                nc.scalar.activation(sd, var, ACT.Sqrt).then_inc(S["std_made"], 1)

            def norm_hi():
                c = 0
                for n in NORM_CHUNKS:
                    wait("hn_made")
                    nc.scalar.activation(xs[:, c:c + n, 0:T], mix[:, 20 + c:20 + c + n, :], ACT.Copy).then_inc(S["hn_hi"], 1)
                    c += n

            def scaled_hi(src, gain, k):
                for b in range(NB):
                    c = NB * k + b
                    ins = nc.scalar.activation(xs[:, c, 0:T], src[:, b, :], ACT.Copy, scale=par[:, PCOL[gain] + c:PCOL[gain] + c + 1])
                ins.then_inc(S["hn_hi"], 1)

            def gate_hi():
                for k in range(4):
                    nc.scalar.activation(g_hi[:, 4 * k:4 * k + 4, :], g_raw[:, 4 * k:4 * k + 4, :], ACT.Copy)\
                        .then_inc(S["gate_hi"], 1)

            def gate_half(ps):
                wait("gate_ps")
                nc.scalar.activation(act_out[:, 0, :], PS[:, ps + 3, T:2 * T], ACT.Copy).then_inc(S["gate_half"], 1)

            def log_sigmoid_parts(src, dst, made):
                steps.do(nc.scalar.activation(dst, src, ACT.Abs))
                steps.do(nc.scalar.activation(dst, dst, ACT.Exp, scale=-1.0))
                nc.scalar.activation(dst, dst, ACT.Ln, bias=1.0).then_inc(S[made], 1)

            act.dma_start(par_rows[0:KC, 0, :], a["mix_norm_g"].rearrange("a (r d) -> (a r) d", d=P))\
                .then_inc(S["gain_loaded"], 16)
            wait("gain_made")
            for k in range(4):
                wait("x_turned")
                scaled_hi(x_turned(k), "mix_norm_g", k)
                nc.scalar.activation(xT[:, NB * k:NB * k + NB, :], x_turned(k), ACT.Copy).then_inc(S["x_copied"], 1)
                act.wait_ge(w_full[k], 16)
                act.wait_ge(w_used, k + 1)
                nc.scalar.activation(w_hi[:, k, :, :], w_raw[:, k, :, :], ACT.Copy).then_inc(hi_made, 1)

            def in1_norm(n, j):
                if (n, j) == (0, 2):
                    wait("x_copied", 4)
                    squares(xT, mix)
                if (n, j) == (0, 3):
                    wait("par_made", 2)
                    nc.scalar.activation(c_act[:, :], par[:, PCOL["c_2"]:PCOL["c_2"] + KC], ACT.Silu).then_inc(S["cact_made"], 1)
                if (n, j) == (0, 3):
                    wait("gate_loaded", 16 * 6)
                    gate_hi()
                if (n, j) == (0, 5):
                    std(in1_rstd, in1_rstd)
                if (n, j) == (1, 2):
                    gate_half(spare("in1a", 1))
                if (n, j) == (1, 3):
                    wait("gate_sum")
                    log_sigmoid_parts(mix[:, 72, :], mix[:, 73, :], "gate_ln")

            stream("in1a", side=in1_norm)

            def copy_values(blk, ps):
                wait("v_turned")
                nc.scalar.activation(mixcols(blk, 2 * STRIP), PS[:, ps:ps + 2, :].rearrange("p b n -> p (b n)"), ACT.Copy)\
                    .then_inc(S["v_copied"], 1)

            def split_upper(c, blk, x=xs):
                nc.scalar.activation(x[:, c:c + 4, 0:T], mix[:, blk:blk + 4, :], ACT.Copy).then_inc(S["y_hi"], 1)

            def fox_exp(h):
                l, st = fox_l(h), fox_stat(h)
                wait("f_max")
                nc.scalar.activation(l[:, 0:P], l[:, 0:P], ACT.Exp, bias=st[:, 2:3], accum_out=st[:, 4:5])
                nc.scalar.activation(l[:, P:3 * P], l[:, P:3 * P], ACT.Exp, bias=st[:, 3:4], accum_out=st[:, 5:6])\
                    .then_inc(S["f_exp"], 1)

            def mlstm_std():
                wait("m_var")
                nc.scalar.activation(m_sd, m_sd, ACT.Sqrt).then_inc(S["m_std"], 1)

            def mixers1(n, j):
                ps = spare("in1b", n)
                if n in FOX_SUMS:
                    f = FOX_SUMS[n]
                    if j == 2:
                        act.wait_ge(evac_done, layers["in1b"].n0 + n + 2)
                        for e in range(2):
                            nc.scalar.activation(fox_sq[:, NB * e:NB * e + NB, :],
                                                 mix[:, 32 + 8 * e + NB * f:36 + 8 * e + NB * f, :], ACT.Square)\
                                .then_inc(S["f_sq"], 1)
                    if j == 5:
                        wait("f_var")
                        nc.scalar.activation(fox_rstd, fox_rstd, ACT.Sqrt).then_inc(S["f_std"], 1)
                if n in FOX_NORM and j == 1:
                    wait("f_rows")
                    nc.scalar.activation(fox_rows, PS[0:2 * NB, ps, 0:T], ACT.Copy).then_inc(S["f_rows_copied"], 1)
                if n in V_TURN and j == (3 if n in MLSTM else 4):
                    copy_values(V_TURN[n], ps + 2)
                if n in FOX_PAIR:
                    h = 2 * FOX_PAIR[n]
                    if j in (2, 3):
                        fox_exp(h + j - 2)
                    if j == 5:
                        for e in range(2):
                            wait("f_turned")
                            nc.scalar.activation(fox_lT(h + e), PS[:, ps + e, 0:3 * P], ACT.Copy).then_inc(S["f_copied"], 1)
                    if j == 6:
                        wait("f_out")
                        nc.scalar.activation(mix[:, 32 + h:34 + h, :].rearrange("p b t -> p (b t)"), PS[:, ps + 2, :], ACT.Copy)\
                            .then_inc(S["f_ready"], 1)
                if n in MLSTM:
                    h = MLSTM[n]
                    if j == 2:
                        wait("m_masked")
                        nc.scalar.activation(m_w, m_w, ACT.Exp).then_inc(S["m_exp"], 1)
                    if j == 4:
                        wait("m_num")
                        nc.scalar.activation(m_e, PS[:, ps + 3, T:2 * T], ACT.Exp).then_inc(S["m_floor"], 1)
                    if j == 6:
                        wait("m_h")
                        nc.scalar.activation(m_sq, mix[:, 2 * h:2 * h + 2, :], ACT.Square).then_inc(S["m_sq"], 1)
                if n in MLSTM_NORM and j == 3:
                    mlstm_std()
                if n == 9 and j in (4, 6):
                    split_upper(2 * (j - 4), 32 + 2 * (j - 4), xf)
                if n == 11 and j == 5:
                    act.wait_ge(evac_done, layers["in1b"].n0 + n + 2)
                    nc.scalar.activation(mix[:, 24:28, :], mix[:, 24:28, :], ACT.Sigmoid).then_inc(S["m_og"], 1)

            def mixers1_end(n, j):
                if (n, j) == (0, 2):
                    mlstm_std()
                if (n, j) == (0, 4):
                    wait("m_y")
                    split_upper(4, 4)
                squares_beside("out1", xT)(n, j)

            stream("in1b", side=mixers1)
            act.wait_ge(w_used, RING + layers["in1b"].end_g)
            wait("m_y")
            split_upper(0, 0)
            all_out("in1b")
            nc.scalar.activation(mix[:, 28:32, :], mix[:, 28:32, :], ACT.Sigmoid).then_inc(S["m_og"], 1)
            stream("out1", side=mixers1_end)
            all_out("out1")
            strip_squares(xT, 3)
            preload(ACT.Sqrt)
            std()
            norm_hi()

            def hidden(func, at, base):
                def piece(layer, i, s, j):
                    if s == 0 and j == 4:
                        act.wait_ge(evac_done, layer.strip(i, 0) + 3)
                        nc.scalar.activation(act_out[:, :, :], act_out[:, :, :], func).then_inc(S["gelu_made"], 1)
                    if s == 1 and j == at:
                        act.wait_ge(S["h2_made"], i + (base + 1))
                        nc.scalar.activation(hs[:, bass.ds(i * NB, NB), 0:T], half[:, :, :], ACT.Copy).then_inc(S["h2_hi"], 1)
                return piece

            def down_side(name, src, up, piece, *gain):
                beside = squares_beside(name, src, *gain)

                def side(n, j):
                    if n == 0 and j < layers[up].G:
                        piece(layers[up], layers[up].pairs - 1, 1, j)
                    beside(n, j)
                return side

            up1_piece = hidden(ACT.Gelu, 1, 0)
            stream("up1", piece=up1_piece)
            down1_side = down_side("down1", xT, "up1", up1_piece)

            def down1_beside(n, j):
                down1_side(n, j)
                if n and j == 3:
                    scaled_hi(xT[:, NB * (n - 1):NB * n, :], "ple_norm_g", n - 1)

            stream("down1", side=down1_beside)

            all_out("down1")
            act.dma_start(mixcols(76, 2 * 256).rearrange("p (t d) -> p t d", t=2),
                          a["p"][0, 0].rearrange("(t p) d -> p t d", p=P)).then_inc(S["p_loaded"], 16)
            scaled_hi(xT[:, 12:16, :], "ple_norm_g", 3)
            strip_squares(xT, 3)

            def gate_sigmoid(k):
                if k < 3:
                    wait("gs_made")
                else:
                    all_out("gate1b")
                g = ple_gate[:, NB * k:NB * k + NB, :]
                nc.scalar.activation(g, g, ACT.Sigmoid).then_inc(S["sig_made"], 1)

            def gate1a_side(n, j):
                if (n, j) == (0, 2):
                    std()
                if (n, j) == (0, 5):
                    wait("p_turned")
                    nc.scalar.activation(ps_in[:, :, 0:T], PS[:, spare("gate1a", 0), :].rearrange("p (c t) -> p c t", t=T), ACT.Copy)\
                        .then_inc(S["p_hi"], 1)
                if (n, j) == (1, 2):
                    gate_sigmoid(0)

            def gate1b_side(n, j):
                if (n, j) == (0, 0):
                    gate_sigmoid(1)
                if (n, j) == (0, 2):
                    wait("gate2_loaded", 16)
                    gate_hi()
                if (n, j) == (0, 4):
                    wait("embedded")
                    strip_squares(xT, 0)
                if (n, j) == (1, 1):
                    wait("embedded")
                    strip_squares(xT, 1)
                if (n, j) == (1, 2):
                    gate_sigmoid(2)
                if (n, j) == (1, 5):
                    wait("embedded")
                    strip_squares(xT, 2)
                if (n, j) == (1, 7):
                    preload(ACT.Sigmoid)

            stream("gate1a", side=gate1a_side)
            stream("proj")
            stream("gate1b", side=gate1b_side)
            gate_sigmoid(3)

            wait("embedded")
            strip_squares(xT, 3)
            preload(ACT.Sqrt)
            std()
            norm_hi()

            def mixers2(n, j):
                ps = spare("in2", n)
                if (n, j) == (1, 2):
                    gate_half(ps)
                if (n, j) == (1, 5):
                    wait("g_pre", GH)
                    log_sigmoid_parts(g_cum, mix[:, 76:80, :], "g_ln")
                if n in GLA_DECAY and j == 1:
                    wait("g_arg")
                    nc.scalar.activation(g_qk, g_qk, ACT.Exp, scale=1.0 / GATE_TAU).then_inc(S["g_decay"], 1)
                if n in GLA_TURN and j == 2:
                    copy_values(GLA_TURN[n], ps + 2)
                if n in GLA_NORM and j == 3:
                    wait("g_var")
                    nc.scalar.activation(g_sd, g_sd, ACT.Sqrt).then_inc(S["g_std"], 1)
                if n in GLA_HEAD and j == 5:
                    h = GLA_HEAD[n]
                    wait("g_out")
                    nc.scalar.activation(g_sq.rearrange("p b t -> p (b t)"), PS[:, ps + 1, :], ACT.Square).then_inc(S["g_sq"], 1)
                    nc.scalar.activation(mixcols(48 + 2 * h, 2 * T), PS[:, ps + 1, :], ACT.Copy).then_inc(S["g_o"], 1)
                if n == 11 and j in (1, 2):
                    wait("c_y")
                    split_upper(0, NB * (j - 1), cf[j - 1])
                if (n, j) == (11, 3):
                    act.wait_ge(evac_done, layers["in2"].n0 + n + 2)
                    nc.scalar.activation(mix[:, 40:44, :], mix[:, 40:44, :], ACT.Silu).then_inc(S["r_silu"], 1)

            stream("in2", side=mixers2)
            act.wait_ge(w_used, RING + layers["in2"].end_g)
            wait("g_y")
            split_upper(8, 48)
            all_out("in2")
            nc.scalar.activation(mix[:, 44:48, :], mix[:, 44:48, :], ACT.Silu).then_inc(S["r_silu"], 1)
            wait("g_y")
            split_upper(12, 52)

            stream("out2", side=squares_beside("out2", mixed, gate_m))
            last_squares("out2")
            preload(ACT.Sqrt)
            std()
            scale_last(mixed, gate_m)
            squares(xT, mix[:, 40:56, :], "mixed")
            std()
            norm_hi()

            up2_piece = hidden(ACT.Silu, 4, layers["up1"].pairs)
            stream("up2", piece=up2_piece)
            stream("down2", side=down_side("down2", y2, "up2", up2_piece, gate_f, "gain_f"))
            last_squares("down2")
            preload(ACT.Sqrt)
            std()
            wait("gain_f")
            scale_last(y2, gate_f)
            for k in range(4):
                wait("y_turned")
                nc.scalar.activation(y_rows[:, :, k * STRIP:(k + 1) * STRIP], PS[:, 2 * k:2 * k + 2, :], ACT.Copy)\
                    .then_inc(S["y_copied"], 1)

        @block.vector
        def _(dve):
            steps = Steps(dve, S["dve_step"])
            tally = Tally()
            V = nc.vector

            def wait(name, by=1):
                dve.wait_ge(S[name], tally.next(name, by))

            def mod_tile(strip, k):
                if k == 0:
                    dve.wait_ge(mod_read, strip + 1)
                slot = k % MOD_RING
                dve.wait_ge(mod_full[slot], strip * (16 * KC // MOD_RING) + 16 * (k // MOD_RING + 1))
                w = mod_w[:, slot, :]
                dve.wait_ge(mod_used, strip * KC + (k + MOD_RING))
                if k == 0:
                    V.tensor_scalar(mod_acc[:, :], w, c_act[:, 0:1], None, ALU.mult).then_inc(mod_used, 1)
                else:
                    V.scalar_tensor_tensor(mod_acc[:, :], w, c_act[:, k:k + 1], mod_acc[:, :], ALU.mult, ALU.add)\
                        .then_inc(mod_used, 1)

            def mod_copy(strip, bank):
                dve.wait_ge(mod_sum, strip + 1)
                V.tensor_copy(modT[:, bass.ds(strip * NB, NB)], PS[:, bank, 0:NB]).then_inc(mod_read, 1)

            def split_lo(layer, i, s, j):
                slot = layer.slot_int(i, s, j) if layer.unrolled else layer.slot(s, j)
                if isinstance(i, int) and layer.group(i, s, j) + RING >= total_groups:
                    return
                dve.wait_ge(hi_made, layer.group(i, s, j) + RING + 1)
                V.tensor_tensor(w_lo[:, slot, :, :], w_raw[:, slot, :, :], w_hi[:, slot, :, :].bitcast(F32),
                                ALU.subtract).then_inc(lo_made, 1)

            def stream(name, evac, per=0, piece=None, side=None):
                layer = layers[name]

                def pair(i, first=False):
                    for s in range(2):
                        for j in range(layer.G):
                            if j and mod_sum_after(layer, i, s, j - 1) is not None:
                                mod_copy(mod_strip(layer, i, mod_sum_after(layer, i, s, j - 1)), 4 - 4 * s + 3)
                            if j == layer.G - 1:
                                if layer.residual or layer.joins(i, s):
                                    dve.wait_ge(w_used, layer.group(i, s, j) + 1 + RING)
                                else:
                                    dve.wait_ge(half_made, layer.halved(i, s))
                                evac(layer, i, s, PS[:, 4 * ((layer.n0 + s) % 2):4 * ((layer.n0 + s) % 2) + NB, :])
                            split_lo(layer, i, s, j)
                            q, tiles = mod_tiles(layer, i, s, j)
                            for k in tiles:
                                mod_tile(mod_strip(layer, i, q), k)
                            if piece and (s or not first):
                                piece(layer, i if s else i - 1, 1 - s, j)
                            if side:
                                side(2 * i + s, j)

                for_pairs(dve, layer, pair, steps, per, peel=piece is not None)

            def to_blocks(dst, blk0):
                def evac(layer, i, s, ps):
                    if layer.joins(i, s):
                        return
                    V.tensor_tensor(dst[:, bass.ds(i * (2 * NB) + (blk0 + s * NB), NB), :], ps[:, :, 0:T], half[:, :, :], ALU.add)\
                        .then_inc(evac_done, 1)
                return evac

            def every_block(row):
                return row.rearrange("p (b t) -> p b t", b=1).broadcast_to([P, NB, T])

            def to_listed(strips, rstd=None):
                def evac(layer, i, s, ps):
                    blk = strips[2 * i + s][1]
                    if rstd is None:
                        V.tensor_tensor(mix[:, blk:blk + NB, :], ps[:, :, 0:T], half[:, :, :], ALU.add).then_inc(evac_done, 1)
                    else:
                        steps.do(V.tensor_tensor(half[:, :, :], ps[:, :, 0:T], half[:, :, :], ALU.add))
                        V.tensor_tensor(mix[:, blk:blk + NB, :], half[:, :, :], every_block(rstd), ALU.mult)\
                            .then_inc(evac_done, 1)
                return evac

            def to_residual(layer, i, s, ps):
                x = xT[:, bass.ds(i * (2 * NB) + s * NB, NB), :]
                if layer.joins(i, s):
                    V.tensor_tensor(x, x, ps[:, :, 0:T], ALU.add).then_inc(evac_done, 1)
                    return
                steps.do(V.tensor_tensor(x, x, ps[:, :, 0:T], ALU.add))
                V.tensor_tensor(x, x, ps[:, :, T:2 * T], ALU.add).then_inc(evac_done, 1)

            def fold_squares():
                wait("strip_sq")
                steps.do(V.tensor_tensor(act_out[:, 0:2, :], act_out[:, 0:2, :], act_out[:, 2:4, :], ALU.add))
                V.tensor_tensor(act_out[:, 0, :], act_out[:, 0, :], act_out[:, 1, :], ALU.add).then_inc(S["sq_folded"], 1)

            def strip_sum(k, ps):
                wait("ss_made")
                if k == 0:
                    V.tensor_copy(ssum[:, :], ps).then_inc(S["ss_read"], 1)
                else:
                    dve.wait_ge(S["ss_read"], tally["ss_own"])
                    V.tensor_tensor(ssum[:, :], ssum[:, :], ps, ALU.add).then_inc(S["ss_read"], 1)
                tally.next("ss_own")
                if k == 2:
                    dve.wait_ge(S["ss_read"], tally["ss_own"])
                    steps.do(V.tensor_scalar(ssum[:, :], ssum[:, :], 1.0 / D, EPS, ALU.mult, ALU.add))

            def sums_beside(name):
                def side(n, j):
                    if n and j == 2:
                        fold_squares()
                    if n and j == 4:
                        strip_sum(n - 1, PS[:, spare(name, n) + 3, 0:T])
                return side

            def mean_square(total, var=mix[:, 36, :]):
                V.tensor_scalar(var, total, 1.0 / D, EPS, ALU.mult, ALU.add).then_inc(S["var_made"], 1)

            def last_mean_square(ps):
                wait("ss_made")
                V.scalar_tensor_tensor(mix[:, 36, :], ps, 1.0 / D, ssum[:, :], ALU.mult, ALU.add).then_inc(S["var_made"], 1)

            def rstd(sd=mix[:, 37, :]):
                wait("std_made")
                steps.do(V.reciprocal(sd, sd))

            def scaled_lo(src, gain, k):
                wait("hn_hi")
                for b in range(NB):
                    c = NB * k + b
                    ins = V.scalar_tensor_tensor(xs[:, c, T:2 * T], src[:, b, :], par[:, PCOL[gain] + c:PCOL[gain] + c + 1],
                                                 xs[:, c, 0:T].bitcast(F32), ALU.mult, ALU.subtract)
                ins.then_inc(S["x_ready"], 1)

            def norm_apply(gain, shift=None):
                def lo(c, n):
                    wait("hn_hi")
                    V.tensor_tensor(xs[:, c:c + n, T:2 * T], mix[:, 20 + c:20 + c + n, :],
                                    xs[:, c:c + n, 0:T].bitcast(F32), ALU.subtract).then_inc(S["x_ready"], 1)

                c0, last = 0, None
                for n in NORM_CHUNKS:
                    for c in range(c0, c0 + n):
                        ins = V.scalar_tensor_tensor(mix[:, 20 + c, :], xT[:, c, :], gain[:, c:c + 1], mix[:, 37, :],
                                                     ALU.mult, ALU.mult)
                    if shift is not None:
                        steps.do(ins)
                        for c in range(c0, c0 + n):
                            ins = V.tensor_scalar(mix[:, 20 + c, :], mix[:, 20 + c, :], shift[:, c:c + 1], None, ALU.add)
                    ins.then_inc(S["hn_made"], 1)
                    if last:
                        lo(*last)
                    last = (c0, n)
                    c0 += n
                lo(*last)

            def pcols(name, n=KC):
                return par[:, PCOL[name]:PCOL[name] + n]

            def gate_lo():
                for k in range(4):
                    wait("gate_hi")
                    V.tensor_tensor(g_lo[:, 4 * k:4 * k + 4, :], g_raw[:, 4 * k:4 * k + 4, :],
                                    g_hi[:, 4 * k:4 * k + 4, :].bitcast(F32), ALU.subtract).then_inc(S["gate_lo"], 1)

            def gate_add(ps):
                wait("gate_half")
                steps.do(V.tensor_tensor(mix[:, 72, :], PS[:, ps + 3, 0:T], act_out[:, 0, :], ALU.add))

            wait("gain_turned")
            V.tensor_copy(par[:, 0:KC], PS[:, 3, 0:KC]).then_inc(S["gain_made"], 1)
            wait("gain_made")
            for k in range(4):
                dve.wait_ge(S["x_copied"], k + 1)
                scaled_lo(x_turned(k), "mix_norm_g", k)
                dve.wait_ge(hi_made, k + 1)
                V.tensor_tensor(w_lo[:, k, :, :], w_raw[:, k, :, :], w_hi[:, k, :, :].bitcast(F32), ALU.subtract)\
                    .then_inc(lo_made, 1)

            def in1_norm(n, j):
                if (n, j) == (0, 2):
                    wait("par_turned")
                    V.tensor_copy(par[:, KC:512], PS[:, 4, KC:512]).then_inc(S["par_made"], 1)
                    V.tensor_copy(par[:, 512:N_PAR], PS[:, 5, 0:N_PAR - 512]).then_inc(S["par_made"], 1)
                    wait("par_made", 2)
                    V.scalar_tensor_tensor(fox_qk_g[:, :], pcols("fox_q_g", 1), FD ** -0.5, pcols("fox_k_g", 1),
                                           ALU.mult, ALU.mult)
                if (n, j) == (0, 4):
                    wait("cact_made")
                    gate_lo()
                    dve.wait_ge(S["gate_lo"], 4)
                    wait("ss_made")
                    mean_square(PS[:, spare("in1a", 0) + 2, 0:T], in1_rstd)
                if (n, j) == (0, 6):
                    rstd(in1_rstd)
                if (n, j) == (1, 2):
                    gate_add(spare("in1a", 1))
                    steps.do(V.tensor_tensor(mix[:, 72, :], mix[:, 72, :], in1_rstd, ALU.mult))
                    V.tensor_scalar(mix[:, 72, :], mix[:, 72, :], gbias[:, 0:1], None, ALU.add).then_inc(S["gate_sum"], 1)
                    steps.mark(V.memset(mix[:, 74, :], 1.0))
                if (n, j) == (1, 5):
                    wait("gate_sum")
                    wait("gate_ln")
                    steps.do(V.scalar_tensor_tensor(mix[:, 73, :], mix[:, 72, :], 0.0, mix[:, 73, :], ALU.min, ALU.subtract))
                    steps.do(V.tensor_tensor_scan(mix[:, 75, :], mix[:, 74, :], mix[:, 73, :], 0.0, ALU.mult, ALU.add))
                    steps.mark(V.tensor_copy(mix[0:MH, 76, :], mix[32:32 + MH, 75, :]))
                    steps.mark(V.tensor_copy(f_F, mix[64:64 + FH, 75, :]))
                    steps.do(V.tensor_scalar(f_negF, mix[64:64 + FH, 75, :], -1.0, None, ALU.mult))
                    steps.do(V.tensor_tensor(m_u, mix[0:MH, 72, :], mix[0:MH, 76, :], ALU.subtract))
                    steps.do(V.tensor_tensor_scan(mix[0:MH, 78, :], m_u, m_u, 0.0, ALU.max, ALU.max))
                    steps.do(V.tensor_scalar(m_negM, mix[0:MH, 78, :], -1.0, None, ALU.mult))
                    V.tensor_tensor(m_negFM, m_negM, mix[0:MH, 76, :], ALU.subtract).then_inc(S["gates_ready"], 1)

            stream("in1a", to_listed(in1_strips, in1_rstd), side=in1_norm)

            def split_rest(c, blk, x=xs):
                wait("y_hi")
                V.tensor_tensor(x[:, c:c + 4, T:2 * T], mix[:, blk:blk + 4, :], x[:, c:c + 4, 0:T].bitcast(F32),
                                ALU.subtract).then_inc(S["x_ready"], 1)

            def fox_max(h, ps):
                l, st = fox_l(h), fox_stat(h)
                wait("f_logits")
                if h >= 2:
                    dve.wait_ge(S["f_turned"], h - 1)
                fs = PS[:, ps + 2 - h % 2, (h % 2) * T:(h % 2 + 1) * T]
                rq = [fox_rstd[:, t * 2 * NB + h % NB:t * 2 * NB + h % NB + 1] for t in range(2)]
                steps.mark(V.scalar_tensor_tensor(l[:, 0:P], fs[:, 0:P], f_col(0, h), causal[:, :], ALU.add, ALU.add))
                steps.mark(V.tensor_scalar(l[:, P:2 * P], fs[:, 0:P], f_col(1, h), None, ALU.add))
                steps.do(V.scalar_tensor_tensor(l[:, 2 * P:3 * P], fs[:, P:2 * P], f_col(1, h), causal[:, :], ALU.add, ALU.add))
                steps.mark(V.scalar_tensor_tensor(l[:, 0:P], PS[:, ps, 0:P], rq[0], l[:, 0:P], ALU.mult, ALU.add))
                steps.do(V.scalar_tensor_tensor(l[:, P:3 * P], PS[:, ps, P:3 * P], rq[1], l[:, P:3 * P], ALU.mult, ALU.add))
                steps.mark(V.tensor_reduce(st[:, 0:1], l[:, 0:P], AX_X, ALU.max))
                steps.do(V.tensor_reduce(st[:, 1:2], l[:, P:3 * P], AX_X, ALU.max))
                V.tensor_scalar(st[:, 2:4], st[:, 0:2], -1.0, None, ALU.mult).then_inc(S["f_max"], 1)

            def fox_weights(h):
                l, st = fox_l(h), fox_stat(h)
                wait("f_exp")
                steps.do(V.reciprocal(st[:, 6:8], st[:, 4:6]))
                V.tensor_scalar(l[:, 0:P], l[:, 0:P], st[:, 6:7], None, ALU.mult)
                V.tensor_scalar(l[:, P:3 * P], l[:, P:3 * P], st[:, 7:8], None, ALU.mult).then_inc(S["f_probs"], 1)

            def mlstm_var(ps):
                wait("m_ss")
                V.tensor_scalar(m_sd, PS[:, ps + 3, 0:T], 1.0 / MD, EPS, ALU.mult, ALU.add).then_inc(S["m_var"], 1)

            def mlstm_norm(h):
                wait("m_std")
                steps.do(V.reciprocal(m_sd, m_sd))
                for v in range(2):
                    y, g = mix[:, 2 * h + v, :], PCOL["mlstm_out_g"] + 2 * h + v
                    steps.mark(V.scalar_tensor_tensor(y, y, par[:, g:g + 1], m_sd, ALU.mult, ALU.mult))
                steps.wait()

            def mlstm_gate(f):
                wait("m_og")
                y = mix[:, NB * f:NB * f + NB, :]
                V.tensor_tensor(y, y, mix[:, 24 + NB * f:28 + NB * f, :], ALU.mult).then_inc(S["m_y"], 1)

            def mixers1(n, j):
                ps = spare("in1b", n)
                if n in FOX_SUMS and j == 4:
                    wait("f_ss")
                    V.tensor_scalar(fox_rstd, PS[:, ps + 3, 0:4 * NB], 1.0 / FD, EPS, ALU.mult, ALU.add).then_inc(S["f_var"], 1)
                if n in FOX_SUMS and j == 6:
                    wait("f_std")
                    V.reciprocal(fox_rstd, fox_rstd).then_inc(S["f_rstd"], 1)
                if n in FOX_NORM and j == 3:
                    wait("f_spread")
                    b = 40 + NB * FOX_NORM[n]
                    V.scalar_tensor_tensor(mixcols(b, NB * T), mixcols(b, NB * T), fox_qk_g[:, 0:1],
                                           PS[:, ps:ps + 2, :].rearrange("p b n -> p (b n)"), ALU.mult, ALU.mult)\
                        .then_inc(S["f_normed"], 1)
                if (n, j) == (0, 2):
                    wait("cols_turned")
                    V.tensor_copy(gate_cols, PS[:, ps, 0:2 * (FH + MH)]).then_inc(S["cols_made"], 1)
                if n in FOX_PAIR:
                    h = 2 * FOX_PAIR[n]
                    if j in (1, 2):
                        fox_max(h + j - 1, ps + j - 1)
                    if j == 3:
                        fox_weights(h)
                        fox_weights(h + 1)
                if n in MLSTM_NORM and j == 2:
                    mlstm_var(ps)
                if n in MLSTM:
                    h = MLSTM[n]
                    if j == 1:
                        wait("m_arg")
                        V.scalar_tensor_tensor(m_w[:, 0:P], PS[:, ps + 1, 0:P], u_col(0, h), causalT[:, :], ALU.add, ALU.add)
                        V.tensor_scalar(m_w[:, P:2 * P], PS[:, ps + 1, P:2 * P], u_col(0, h), None, ALU.add)
                        V.scalar_tensor_tensor(m_w[:, 2 * P:3 * P], PS[:, ps + 1, P:2 * P], u_col(1, h), causalT[:, :],
                                               ALU.add, ALU.add).then_inc(S["m_masked"], 1)
                    if j == 2:
                        wait("m_exp")
                        V.scalar_tensor_tensor(m_sw, PS[:, ps, 0:3 * P], MD ** -0.5, m_w, ALU.mult, ALU.mult)\
                            .then_inc(S["m_weighed"], 1)
                    if j == 4:
                        wait("m_num")
                        wait("m_floor")
                        steps.do(V.scalar_tensor_tensor(m_e, PS[:, ps + 3, 0:T], -1.0, m_e, ALU.mult, ALU.max))
                        steps.do(V.tensor_tensor(m_e, PS[:, ps + 3, 0:T], m_e, ALU.max))
                        steps.do(V.reciprocal(m_e, m_e))
                        for v in range(2):
                            ins = V.tensor_tensor(mix[:, 2 * h + v, :], PS[:, ps + 2, v * T:(v + 1) * T], m_e, ALU.mult)
                        ins.then_inc(S["m_h"], 1)
                if n in MLSTM_NORM and j == 5:
                    mlstm_norm(MLSTM_NORM[n])
                if n == 9 and j in (4, 6):
                    split_rest(2 * (j - 4), 32 + 2 * (j - 4), xf)
                if n == 11 and j == 6:
                    mlstm_gate(0)

            def mixers1_end(n, j):
                if (n, j) == (0, 1):
                    mlstm_var(spare("out1", 0))
                if (n, j) == (0, 2):
                    mlstm_norm(MH - 1)
                    mlstm_gate(1)
                if (n, j) == (0, 4):
                    split_rest(4, 4)
                sums_beside("out1")(n, j)

            stream("in1b", to_listed(in1_strips[2:], in1_rstd), side=mixers1)
            split_rest(0, 0)
            stream("out1", to_residual, side=mixers1_end)
            fold_squares()
            last_mean_square(PS[:, spare("out1", 3) + 3, 0:T])
            rstd()
            norm_apply(pcols("ffn_norm_g"))

            def conv(src, dst, lag, bias=False):
                for b in range(NB):
                    w = conv_p[:, 2 - lag, b:b + 1]
                    if lag:
                        ins = V.scalar_tensor_tensor(dst[:, b, lag:T], src[:, b, 0:T - lag], w, dst[:, b, lag:T],
                                                     ALU.mult, ALU.add)
                    elif bias:
                        ins = V.tensor_scalar(dst[:, b, :], src[:, b, :], w, conv_p[:, 3, b:b + 1], ALU.mult, ALU.add)
                    else:
                        ins = V.tensor_scalar(dst[:, b, :], src[:, b, :], w, None, ALU.mult)
                return ins

            def conv_params(name, first, n_rows, stride):
                src = par[:, PCOL[name]:PCOL[name] + n_rows * stride].rearrange("p (w f) -> p w f", f=stride)
                steps.do(V.tensor_copy(conv_p[:, 0:n_rows, :], src[:, :, bass.ds(first, NB)]))

            def hidden_product(i, base, gate):
                dve.wait_ge(S["gelu_made"], i + (base + 1))
                V.tensor_tensor(half[:, :, :], act_out[:, :, :], gate, ALU.mult).then_inc(S["h2_made"], 1)

            def hidden_lo(i, base):
                dve.wait_ge(S["h2_hi"], i + (base + 1))
                h = hs[:, bass.ds(i * NB, NB), :]
                V.tensor_tensor(h[:, :, T:2 * T], half[:, :, :], h[:, :, 0:T].bitcast(F32), ALU.subtract).then_inc(evac_done, 1)

            def join_halves(layer, i, s, ps):
                steps.do(V.tensor_tensor(half[:, :, :], ps[:, :, 0:T], half[:, :, :], ALU.add))

            def up1_piece(layer, i, s, j):
                if s == 0 and j == 0:
                    conv_params("conv_w", i * NB, 4, FB)
                if s == 0 and j < 2:
                    steps.do(conv(half, act_out, j, bias=True))
                if s == 0 and j == 2:
                    conv(half, act_out, j).then_inc(evac_done, 1)
                if s == 1 and j == 0:
                    hidden_product(i, 0, half[:, :, :])
                if s == 1 and j == 2:
                    hidden_lo(i, 0)

            stream("up1", join_halves, 5, up1_piece)

            def down_side(name, up, piece):
                beside = sums_beside(name)

                def side(n, j):
                    if n == 0 and j < layers[up].G:
                        piece(layers[up], layers[up].pairs - 1, 1, j)
                    beside(n, j)
                return side

            down1_side = down_side("down1", "up1", up1_piece)

            def down1_beside(n, j):
                down1_side(n, j)
                if n and j == 3:
                    scaled_lo(xT[:, NB * (n - 1):NB * n, :], "ple_norm_g", n - 1)

            stream("down1", to_residual, side=down1_beside)
            scaled_lo(xT[:, 12:16, :], "ple_norm_g", 3)
            fold_squares()

            def gate1a_side(n, j):
                if (n, j) == (0, 1):
                    last_mean_square(PS[:, spare("gate1a", 0) + 3, 0:T])
                if (n, j) == (0, 3):
                    rstd()
                if (n, j) == (0, 5):
                    wait("p_hi")
                    V.tensor_tensor(ps_in[:, :, T:2 * T], PS[:, spare("gate1a", 0), :].rearrange("p (c t) -> p c t", t=T),
                                    ps_in[:, :, 0:T].bitcast(F32), ALU.subtract).then_inc(S["p_ready"], 1)

            def to_gate(first):
                def evac(layer, i, s, ps):
                    k = 2 * i + s + first
                    g = ple_gate[:, NB * k:NB * k + NB, :]
                    if layer.joins(i, s):
                        V.tensor_tensor(g, ps[:, :, 0:T], every_block(mix[:, 37, :]), ALU.mult).then_inc(evac_done, 1)
                        return
                    V.tensor_tensor(g, ps[:, :, 0:T], half[:, :, :], ALU.add).then_inc(evac_done, 1)
                    dve.wait_ge(evac_done, layer.strip(i, s) + 3)
                    V.tensor_tensor(g, g, every_block(mix[:, 37, :]), ALU.mult).then_inc(S["gs_made"], 1)
                return evac

            def embed(k):
                wait("sig_made")
                g, x = ple_gate[:, NB * k:NB * k + NB, :], xT[:, NB * k:NB * k + NB, :]
                steps.do(V.tensor_tensor(g, g, ple_in[:, NB * k:NB * k + NB, :], ALU.mult))
                V.tensor_tensor(x, x, g, ALU.add).then_inc(S["embedded"], 1)

            def gate1b_side(n, j):
                ps = PS[:, spare("gate1b", n) + 3, 0:T]
                if (n, j) == (0, 0):
                    embed(0)
                if (n, j) == (0, 1):
                    embed(1)
                if (n, j) == (0, 3):
                    gate_lo()
                if (n, j) == (0, 4):
                    fold_squares()
                if (n, j) == (0, 6):
                    strip_sum(0, ps)
                if (n, j) == (1, 1):
                    fold_squares()
                if (n, j) == (1, 3):
                    strip_sum(1, ps)
                    embed(2)
                if (n, j) == (1, 5):
                    fold_squares()

            stream("gate1a", to_gate(0), side=gate1a_side)
            stream("proj", to_blocks(mix, 40), 0)
            stream("gate1b", to_gate(2), side=gate1b_side)
            strip_sum(2, PS[:, spare("gate1b", 1) + 3, 0:T])
            embed(3)
            fold_squares()

            n_m = 3 * KC
            dve.wait_ge(mod_read, 1 + n_m // NB)
            steps.do(V.tensor_tensor(modT[:, 0:n_m], modT[:, 0:n_m], pcols("b_mod_2", n_m), ALU.add))
            steps.mark(V.scalar_tensor_tensor(scale_m, scale_m, 1.0, pcols("mix_pre_w_2"), ALU.add, ALU.mult))
            steps.do(V.tensor_tensor(gate_m, gate_m, pcols("mix_post_w_2"), ALU.mult))
            last_mean_square(PS[:, spare("gate1b", 1) + 2, 0:T])
            rstd()
            norm_apply(scale_m, shift_m)

            def gla_decay(h):
                for l in range(8):
                    H = P >> l
                    ev, cv = halves(g_qk[:, l, :], H), halves(g_cum[:, h, :], H)
                    edge = cv[:, :, 0, H - 1:H].broadcast_to([P, T // (2 * H), H])
                    V.tensor_tensor(ev[:, :, 0, :], edge, cv[:, :, 0, :], ALU.subtract)
                    ins = V.tensor_tensor(ev[:, :, 1, :], cv[:, :, 1, :], edge, ALU.subtract)
                ins.then_inc(S["g_arg"], 1)

            def gla_decayed(h):
                wait("g_decay")
                for l in range(8):
                    ev, qv, kv = (halves(v, P >> l) for v in (g_qk[:, l, :], mix[:, 24 + h, :], mix[:, 28 + h, :]))
                    V.tensor_tensor(ev[:, :, 0, :], ev[:, :, 0, :], kv[:, :, 0, :], ALU.mult)
                    ins = V.tensor_tensor(ev[:, :, 1, :], ev[:, :, 1, :], qv[:, :, 1, :], ALU.mult)
                ins.then_inc(S["g_qk"], 1)

            def gla_merge(h, l, ps):
                bank, c0 = gla_place(l)
                if l == 0:
                    V.tensor_copy(g_sc[:, P:2 * P], PS[:, ps, 0:P]).then_inc(S["g_merged"], 1)
                    return
                mask = masks[:, l - 1:l, :] if l < 8 else ident[:, :].rearrange("p (k n) -> p k n", k=1)
                dve.wait_ge(S["g_merged"], 9 * h + l)
                V.copy_predicated(g_sc.rearrange("p (k n) -> p k n", n=P)[:, 0:3:2, :], mask.bitcast(I32).broadcast_to([P, 2, P]),
                                  PS[:, ps + bank, c0:c0 + T].rearrange("p (k n) -> p k n", n=P)).then_inc(S["g_merged"], 1)

            def gla_gate(f):
                wait("r_silu")
                o = mix[:, 48 + NB * f:52 + NB * f, :]
                V.tensor_tensor(o, o, mix[:, 40 + NB * f:44 + NB * f, :], ALU.mult).then_inc(S["g_y"], 1)

            def mixers2(n, j):
                ps = spare("in2", n)
                if (n, j) == (1, 2):
                    gate_add(ps)
                    V.tensor_copy(mix[0:16, 80, :], mix[0:16, 72, :]).then_inc(S["gates_ready"], 1)
                if (n, j) == (1, 4):
                    gb = pcols("gate_b_2", GH)
                    wait("g_lr")
                    for h in range(GH):
                        V.tensor_scalar(g_cum[:, h, :], PS[:, ps + 1 + h // 2, (h % 2) * T:(h % 2 + 1) * T], gb[:, h:h + 1], None,
                                        ALU.add).then_inc(S["g_pre"], 1)
                    steps.mark(V.memset(g_one, 1.0))
                if (n, j) == (1, 7):
                    wait("g_pre", GH)
                    wait("g_ln")
                    steps.do(V.scalar_tensor_tensor(mix[:, 76:80, :], g_cum, 0.0, mix[:, 76:80, :], ALU.min, ALU.subtract))
                    for h in range(GH):
                        steps.mark(V.tensor_tensor_scan(g_cum[:, h, :], g_one, mix[:, 76 + h, :], 0.0, ALU.mult, ALU.add))
                    steps.wait()
                if (n, j) == (1, 3):
                    dve.wait_ge(evac_done, layers["in2"].n0 + n + 2)
                    steps.do(V.tensor_scalar(mix[:, 24:28, :], mix[:, 24:28, :], GDK ** -0.5, None, ALU.mult))
                if n in GLA_DECAY and j == 0:
                    gla_decay(GLA_DECAY[n])
                if n in GLA_DECAY and j == 3:
                    dve.wait_ge(evac_done, layers["in2"].n0 + n + 2)
                    gla_decayed(GLA_DECAY[n])
                if n in GLA_HEAD and j in (1, 3):
                    h = GLA_HEAD[n]
                    if j == 1:
                        steps.do(V.memset(g_sc, 0.0))
                    if (n, j) == (3, 1):
                        wait("masks_made", 21)
                    wait("g_score")
                    for l in range(4) if j == 1 else range(4, 9):
                        gla_merge(h, l, ps)
                if n in GLA_NORM and j == 2:
                    wait("g_ss")
                    V.tensor_scalar(g_sd, PS[:, ps + 3, 0:T], 1.0 / GDV, EPS, ALU.mult, ALU.add).then_inc(S["g_var"], 1)
                if n in GLA_NORM and j == 5:
                    wait("g_std")
                    steps.do(V.reciprocal(g_sd, g_sd))
                    for v in range(2):
                        o, g = mix[:, 48 + 2 * GLA_NORM[n] + v, :], PCOL["gla_norm_w_2"] + v
                        steps.mark(V.scalar_tensor_tensor(o, o, par[:, g:g + 1], g_sd, ALU.mult, ALU.mult))
                    steps.wait()
                if n in CONV_HALF:
                    c0 = NB * CONV_HALF[n]
                    u, y, cw = mix[:, 8 + c0:12 + c0, :], mix[:, 16 + c0:20 + c0, :], pcols("conv_w_2", 24)
                    if j == 4:
                        dve.wait_ge(evac_done, layers["in2"].n0 + n + 2)
                        steps.do(V.tensor_tensor(u, u, y, ALU.mult))
                    if j in (5, 6, 7):
                        lag = j - 5
                        for b in range(NB):
                            w = cw[:, 8 * (2 - lag) + c0 + b:8 * (2 - lag) + c0 + b + 1]
                            if lag:
                                ins = V.scalar_tensor_tensor(y[:, b, lag:T], u[:, b, 0:T - lag], w, y[:, b, lag:T], ALU.mult, ALU.add)
                            else:
                                ins = V.tensor_scalar(y[:, b, :], u[:, b, :], w, None, ALU.mult)
                        steps.do(ins)
                if n == 10 and j in (3, 4):
                    b = NB * (j - 3)
                    dve.wait_ge(evac_done, layers["in2"].n0 + n + 2)
                    V.tensor_tensor(mix[:, b:b + NB, :], mix[:, b:b + NB, :], mix[:, 16 + b:16 + b + NB, :], ALU.mult)\
                        .then_inc(S["c_y"], 1)
                if n == 11 and j in (1, 2):
                    split_rest(0, NB * (j - 1), cf[j - 1])
                if (n, j) == (11, 5):
                    gla_gate(0)

            stream("in2", to_listed(in2_strips), side=mixers2)
            split_rest(8, 48)
            gla_gate(1)
            split_rest(12, 52)

            def add_normed(name, y, made):
                for k in range(4):
                    part = slice(NB * k, NB * k + NB)
                    if k < 3:
                        wait("y_scaled")
                    else:
                        dve.wait_ge(evac_done, 2 + layers[name].end)
                    steps.do(V.tensor_tensor(y[:, part, :], y[:, part, :], every_block(mix[:, 37, :]), ALU.mult))
                    V.tensor_tensor(xT[:, part, :], xT[:, part, :], y[:, part, :], ALU.add).then_inc(S[made], 1)

            dve.wait_ge(mod_read, 1 + layers["down2"].mod)
            part = par[:, PCOL["b_mod_2"] + 3 * KC:PCOL["b_mod_2"] + 5 * KC]
            steps.do(V.tensor_tensor(modT[:, 3 * KC:5 * KC], modT[:, 3 * KC:5 * KC], part, ALU.add))
            steps.do(V.scalar_tensor_tensor(scale_f, scale_f, 1.0, pcols("ffn_pre_w_2"), ALU.add, ALU.mult))
            stream("out2", to_blocks(mix, 16), side=sums_beside("out2"))
            fold_squares()
            last_mean_square(PS[:, spare("out2", 3) + 3, 0:T])
            rstd()
            add_normed("out2", mixed, "mixed")
            wait("ss_made")
            mean_square(PS[:, 0, 0:T])
            rstd()
            norm_apply(scale_f, shift_f)

            def up2_piece(layer, i, s, j):
                base = layers["up1"].pairs
                dst = act_out if s == 0 else conv_tmp
                if j == 0:
                    conv_params("ffn_conv_w_2", i * NB + s * FB, 3, 2 * FB)
                if j < 2 or (j == 2 and s == 1):
                    steps.do(conv(half, dst, j))
                elif j == 2:
                    conv(half, dst, j).then_inc(evac_done, 1)
                if s == 1 and j == 3:
                    hidden_product(i, base, conv_tmp[:, :, :])
                if s == 1 and j == 5:
                    hidden_lo(i, base)

            stream("up2", join_halves, 9, up2_piece)
            down2_side = down_side("down2", "up2", up2_piece)

            def outer_gain(k):
                dve.wait_ge(mod_read, 1 + layers["down2"].mod + k + 1)
                g, b = gate_f[:, NB * k:NB * k + NB], PCOL["b_mod_2"] + 5 * KC + NB * k
                steps.do(V.tensor_tensor(g, g, par[:, b:b + NB], ALU.add))
                V.tensor_tensor(g, g, pcols("ffn_post_w_2")[:, NB * k:NB * k + NB], ALU.mult).then_inc(S["gain_f"], 1)

            def down2_beside(n, j):
                if n and j == 0:
                    outer_gain(n - 1)
                down2_side(n, j)

            stream("down2", to_blocks(y2, 0), side=down2_beside)
            outer_gain(3)
            fold_squares()
            last_mean_square(PS[:, spare("down2", 3) + 3, 0:T])
            rstd()
            add_normed("down2", y2, "res_made")

        @block.tensor
        def _(pe):
            tally = Tally()
            M = nc.tensor.matmul

            def wait(name, by=1):
                pe.wait_ge(S[name], tally.next(name, by))

            def all_out(name):
                pe.wait_ge(evac_done, 2 + layers[name].end)

            def stream(name, x, ready=None, first=0, chunks=(4, 4, 4, 4), side=None):
                layer = layers[name]
                last_k = layer.G * GK - 1
                mods = [l.mod + l.mod_pairs * l.mod_per_pair for l in layers.values() if l.mod is not None and l.g0 < layer.g0]
                if mods:
                    pe.wait_ge(mod_read, max(mods) + 1)

                def pair(i):
                    if layer.mod_pairs not in (0, layer.pairs) and i == layer.mod_pairs:
                        pe.wait_ge(mod_read, layer.mod + layer.mod_pairs * layer.mod_per_pair + 1)
                    for s in range(2):
                        bank = 4 * ((layer.n0 + s) % 2)
                        n = layer.strip(i, s)
                        pe.wait_ge(evac_done, n + 1)
                        if layer.takes_mod(i) and (s == 0 or layer.mod_per_pair > 1):
                            pe.wait_ge(mod_read, mod_strip(layer, i, s) + 1)
                        for j in range(layer.G):
                            slot = layer.slot_int(i, s, j) if layer.unrolled else layer.slot(s, j)
                            pe.wait_ge(lo_made, layer.group(i, s, j) + (1 + RING))
                            if ready is not None and s == 0:
                                for n_chunk in range(len(chunks)):
                                    if sum(chunks[:n_chunk]) == GK * j:
                                        pe.wait_ge(S["x_ready"], ready + n_chunk + 1)
                            for k in range(GK):
                                c = (GK * j + k + first) % (layer.G * GK)
                                for b in range(NB):
                                    def hi(start, stop):
                                        if layer.joins(i, s):
                                            for e in range(2):
                                                ins = M(PS[:, bank + b, 0:T], w_hi[:, slot, k, b * P:(b + 1) * P],
                                                        x(c)[:, e * T:(e + 1) * T], start=start and e == 0, stop=stop and e == 1)
                                            return ins
                                        return M(PS[:, bank + b, :], w_hi[:, slot, k, b * P:(b + 1) * P], x(c),
                                                 start=start, stop=stop)

                                    def lo():
                                        return M(PS[:, bank + b, 0:T], w_lo[:, slot, k, b * P:(b + 1) * P], x(c)[:, 0:T],
                                                 start=False, stop=False)

                                    if GK * j + k < last_k:
                                        hi(j == 0 and k == 0, False)
                                        ins = lo()
                                    else:
                                        lo()
                                        ins = hi(False, True)
                            ins.then_inc(w_used, 1)
                            if mod_sum_after(layer, i, s, j) is not None:
                                strip = mod_strip(layer, i, mod_sum_after(layer, i, s, j))
                                pe.wait_ge(mod_used, strip * KC + (KC + MOD_RING))
                                pe.wait_ge(evac_done, n + 2)
                                for b in range(NB):
                                    ins = M(PS[:, 4 - bank + 3, b:b + 1], mod_acc[:, b * P:(b + 1) * P], ones[:, 0:1],
                                            start=True, stop=True)
                                ins.then_inc(mod_sum, 1)
                            if side:
                                side(2 * i + s, j)

                for_pairs(pe, layer, pair)

            def blocks_of(tile):
                return lambda c: tile[:, c, :]

            def sum_squares(src, c0, n, ps, first=True, last=True):
                for c in range(c0, c0 + n):
                    if c % NB == 0:
                        wait("sq_made")
                    ins = M(ps, ones[:, :], src[:, c, :], start=first and c == c0, stop=last and c == c0 + n - 1)
                if last:
                    ins.then_inc(S["ss_made"], 1)

            def strip_sum(bank):
                wait("sq_folded")
                M(PS[:, bank, 0:T], ones[:, :], act_out[:, 0, :], start=True, stop=True).then_inc(S["ss_made"], 1)

            def sums_beside(name):
                def side(n, j):
                    if n and j == 4:
                        strip_sum(spare(name, n) + 3)
                    if n and j == 6:
                        wait("ss_read")
                return side

            def gate_block(ps):
                wait("gate_lo", 4)
                for c in range(KC - 1):
                    M(PS[:, ps + 3, :], g_hi[:, c, :], xs[:, c, :], start=(c == 0), stop=False)
                    M(PS[:, ps + 3, 0:T], g_lo[:, c, :], xs[:, c, 0:T], start=False, stop=False)
                M(PS[:, ps + 3, 0:T], g_lo[:, KC - 1, :], xs[:, KC - 1, 0:T], start=False, stop=False)
                M(PS[:, ps + 3, :], g_hi[:, KC - 1, :], xs[:, KC - 1, :], start=False, stop=True).then_inc(S["gate_ps"], 1)

            def turn_values(blk, ps):
                for t in range(2):
                    for b in range(NB):
                        ins = nc.tensor.transpose(PS[:, ps + t, b * P:(b + 1) * P], mix[:, blk + b, t * P:(t + 1) * P], ident[:, :])
                ins.then_inc(S["v_turned"], 1)

            def causal_sum(dst, first, second, rhs):
                M(dst[:, 0:P], first, rhs[:, 0:P], start=True, stop=True)
                M(dst[:, P:2 * P], first, rhs[:, P:2 * P], start=True, stop=False)
                return M(dst[:, P:2 * P], second, rhs[:, 2 * P:3 * P], start=False, stop=True)

            TILES = ((0, 0), (0, 1), (1, 1))

            def turn_x(k):
                pe.wait_ge(x_loaded[k], 16)
                if k >= 2:
                    pe.wait_ge(S["x_ready"], k - 1)
                for b in range(NB):
                    for t in range(2):
                        ins = nc.tensor.transpose(x_turned(k)[:, b, t * P:(t + 1) * P],
                                                  x_rows[:, t, (NB * k + b) * P:(NB * k + b + 1) * P], ident[:, :])
                ins.then_inc(S["x_turned"], 1)

            wait("consts", 4)
            wait("gain_loaded", 16)
            nc.tensor.transpose(PS[:, 3, 0:KC], par_rows[0:KC, 0, :], ident[0:KC, 0:KC]).then_inc(S["gain_turned"], 1)
            turn_x(0)
            turn_x(1)
            wait("gain_made")

            def in1_norm(n, j):
                ps = spare("in1a", n)
                if n == 0 and j in (0, 1):
                    turn_x(2 + j)
                if (n, j) == (0, 2):
                    pe.wait_ge(S["x_ready"], 3)
                    wait("par_loaded", 16 * (len(par_pieces()) - 1))
                    for k in range(PAR_TILES):
                        rows = min(P, N_PAR - k * P)
                        ins = nc.tensor.transpose(PS[:, ps + k // 4, (k % 4) * P:(k % 4) * P + rows], par_rows[0:rows, k, :],
                                                  ident[0:rows, 0:rows])
                    ins.then_inc(S["par_turned"], 1)
                if n == 0 and j in (3, 4):
                    pe.wait_ge(S["x_ready"], 4)
                    sum_squares(mix, 8 * (j - 3), 8, PS[:, ps + 2, 0:T], first=j == 3, last=j == 4)
                if (n, j) == (0, 7):
                    wait("var_made")
                    wait("par_made", 2)
                if (n, j) == (1, 1):
                    pe.wait_ge(evac_done, layers["in1a"].n0 + 3)
                    gate_block(ps)
                if (n, j) == (1, 7):
                    wait("gate_sum")

            stream("in1a", blocks_of(xs), ready=0, side=in1_norm)

            def turn_gates(ps):
                for rows, n, c0 in ((f_F, FH, 0), (m_u, MH, 2 * FH)):
                    for t in range(2):
                        ins = nc.tensor.transpose(PS[:, ps, c0 + t * n:c0 + (t + 1) * n], rows[:, t * P:(t + 1) * P],
                                                  ident[0:n, 0:n])
                ins.then_inc(S["cols_turned"], 1)

            def fox_logits(h, ps):
                for e in range(2):
                    M(PS[:, ps + 2, e * T:(e + 1) * T], onehot[0:FH, h + e, :], f_negF, start=True, stop=True)
                for e in range(2):
                    for n, (s, t) in enumerate(TILES):
                        ins = M(PS[:, ps + e, n * P:(n + 1) * P], mix[:, 32 + h + e, t * P:(t + 1) * P],
                                mix[:, 40 + h + e, s * P:(s + 1) * P], start=True, stop=True)
                    ins.then_inc(S["f_logits"], 1)

            def mlstm_scores(h, ps):
                for n, (s, t) in enumerate(TILES):
                    for d in range(2):
                        M(PS[:, ps, n * P:(n + 1) * P], mix[:, 8 + 2 * h + d, s * P:(s + 1) * P],
                          mix[:, 2 * h + d, t * P:(t + 1) * P], start=(d == 0), stop=(d == 1))
                M(PS[:, ps + 1, 0:T], onehot[0:MH, h, :], m_negM, start=True, stop=True).then_inc(S["m_arg"], 1)

            def mlstm_sums(h, ps):
                values = turned_values(16 + NB * (h // 2))
                wait("m_weighed")
                for v in range(2):
                    c0 = (h % 2) * MD + v * P
                    causal_sum(PS[:, ps + 2, v * T:(v + 1) * T], values[:, 0, c0:c0 + P], values[:, 1, c0:c0 + P], m_sw)
                causal_sum(PS[:, ps + 3, 0:T], ones[:, :], ones[:, :], m_sw)
                M(PS[:, ps + 3, T:2 * T], onehot[0:MH, h, :], m_negFM, start=True, stop=True).then_inc(S["m_num"], 1)

            def mlstm_sum_squares(ps):
                wait("m_sq")
                for v in range(2):
                    ins = M(PS[:, ps + 3, 0:T], ones[:, :], m_sq[:, v, :], start=(v == 0), stop=(v == 1))
                ins.then_inc(S["m_ss"], 1)

            def mixers1(n, j):
                ps = spare("in1b", n)
                if j == 1:
                    pe.wait_ge(evac_done, layers["in1b"].n0 + n + 2)
                if (n, j) == (0, 2):
                    wait("gates_ready")
                    turn_gates(ps)
                if n in FOX_SUMS and j == 4:
                    wait("f_sq", 2)
                    for t in range(2):
                        for b in range(2 * NB):
                            ins = M(PS[:, ps + 3, t * 2 * NB + b:t * 2 * NB + b + 1], fox_sq[:, b, t * P:(t + 1) * P],
                                    ones[:, 0:1], start=True, stop=True)
                    ins.then_inc(S["f_ss"], 1)
                if n in FOX_NORM and j == 1:
                    wait("f_rstd")
                    for t in range(2):
                        ins = nc.tensor.transpose(PS[0:2 * NB, ps, t * P:(t + 1) * P],
                                                  fox_rstd[:, t * 2 * NB:(t + 1) * 2 * NB], ident[:, :])
                    ins.then_inc(S["f_rows"], 1)
                if n in FOX_NORM and j == 3:
                    wait("f_rows_copied")
                    for b in range(NB):
                        ins = M(PS[:, ps + b // 2, (b % 2) * T:(b % 2 + 1) * T], onehot[0:2 * NB, NB + b, :], fox_rows,
                                start=True, stop=True)
                    ins.then_inc(S["f_spread"], 1)
                if n in FOX_PAIR:
                    h = 2 * FOX_PAIR[n]
                    if j == 1:
                        fox_logits(h, ps)
                    if j == 5:
                        for e in range(2):
                            wait("f_probs")
                            for k in range(3):
                                ins = nc.tensor.transpose(PS[:, ps + e, k * P:(k + 1) * P], fox_l(h + e)[:, k * P:(k + 1) * P],
                                                          ident[:, :])
                            ins.then_inc(S["f_turned"], 1)
                    if j == 6:
                        values = turned_values(48 + NB * (h // NB))
                        for e in range(2):
                            wait("f_copied")
                            c0 = ((h + e) % NB) * FD
                            ins = causal_sum(PS[:, ps + 2, e * T:(e + 1) * T], values[:, 0, c0:c0 + P], values[:, 1, c0:c0 + P],
                                             fox_lT(h + e))
                        ins.then_inc(S["f_out"], 1)
                if n in MLSTM_NORM and j == 1:
                    mlstm_sum_squares(ps)
                if n in MLSTM:
                    if j == 1:
                        mlstm_scores(MLSTM[n], ps)
                    if j == 4:
                        if n in V_TURN:
                            wait("v_copied")
                        if n in MLSTM_NORM:
                            pe.wait_ge(S["m_var"], MLSTM_NORM[n] + 1)
                        mlstm_sums(MLSTM[n], ps)
                if n in V_TURN and j == (2 if n in MLSTM else 4):
                    if n in FOX_PAIR:
                        pe.wait_ge(S["f_max"], 2 * FOX_PAIR[n] + 2)
                    turn_values(V_TURN[n], ps + 2)
                if j == 5:
                    if n == 0:
                        wait("cols_made")
                    if n in FOX_SUMS:
                        pe.wait_ge(S["f_var"], FOX_SUMS[n] + 1)
                    if n in FOX_NORM:
                        wait("f_normed")
                    if n in FOX_PAIR and n in V_TURN:
                        wait("v_copied")
                if j == layers["in1b"].G - 1:
                    if n in FOX_PAIR:
                        wait("f_ready")
                    if n in MLSTM:
                        wait("m_h")
                    if n in MLSTM_NORM:
                        pe.wait_ge(S["m_var"], MLSTM_NORM[n] + 1)

            def mixers1_end(n, j):
                if (n, j) == (0, 1):
                    pe.wait_ge(evac_done, layers["out1"].n0 + 2)
                    mlstm_sum_squares(spare("out1", 0))
                if (n, j) == (0, layers["out1"].G - 1):
                    pe.wait_ge(S["m_var"], MH)
                sums_beside("out1")(n, j)

            stream("in1b", blocks_of(xs), side=mixers1)
            stream("out1", lambda c: xf[:, c - FOX_OUT, :] if c >= FOX_OUT else xs[:, c, :], ready=4, first=FOX_OUT, side=mixers1_end)

            strip_sum(spare("out1", 3) + 3)
            stream("up1", blocks_of(xs), ready=8, chunks=NORM_CHUNKS)

            def down_side(name, up):
                beside = sums_beside(name)

                def side(n, j):
                    if n == 0 and GK * (j + 1) == FB - NB:
                        pe.wait_ge(evac_done, 2 + layers[up].end)
                    beside(n, j)
                return side

            stream("down1", blocks_of(hs), side=down_side("down1", "up1"))

            def gate1a_side(n, j):
                ps = spare("gate1a", n)
                if (n, j) == (0, 1):
                    strip_sum(ps + 3)
                if (n, j) == (0, 4):
                    wait("p_loaded", 16)
                    p_rows = mixcols(76, 512).rearrange("p (t d) -> p t d", t=2)
                    for c in range(2):
                        for t in range(2):
                            ins = nc.tensor.transpose(PS[:, ps, c * T + t * P:c * T + (t + 1) * P],
                                                      p_rows[:, t, c * P:(c + 1) * P], ident[:, :])
                    ins.then_inc(S["p_turned"], 1)
                if (n, j) == (0, 7):
                    wait("var_made", 2)
                    wait("p_ready")

            def gate1b_side(n, j):
                ps = spare("gate1b", n) + 3
                if j == 1:
                    pe.wait_ge(evac_done, layers["gate1b"].n0 + n + 2)
                if (n, j) in ((0, 6), (1, 3), (1, 7)):
                    strip_sum(ps)
                if (n, j) in ((0, 7), (1, 5)):
                    wait("ss_read")

            stream("gate1a", blocks_of(xs), ready=13, side=gate1a_side)
            stream("proj", blocks_of(ps_in))
            stream("gate1b", blocks_of(xs), side=gate1b_side)
            strip_sum(spare("gate1b", 1) + 2)
            wait("ss_read")

            def mixers2(n, j):
                ps = spare("in2", n)
                if j == 1:
                    pe.wait_ge(evac_done, layers["in2"].n0 + n + 2)
                if (n, j) == (1, 1):
                    gate_block(ps)
                if (n, j) == (1, 4):
                    wait("gates_ready")
                    wait("gw2_loaded", 16)
                    for h in range(GH):
                        ins = M(PS[:, ps + 1 + h // 2, (h % 2) * T:(h % 2 + 1) * T], gate_w2[:, h * GDK:(h + 1) * GDK],
                                mix[0:16, 80, :], start=True, stop=True)
                    ins.then_inc(S["g_lr"], 1)
                if n in GLA_HEAD and j in (1, 3):
                    h = GLA_HEAD[n]
                    if j == 1:
                        wait("g_qk")
                    else:
                        pe.wait_ge(S["g_merged"], 9 * h + 4)
                        if n in GLA_TURN:
                            wait("v_copied")
                    for l in range(4) if j == 1 else range(4, 9):
                        bank, c0 = gla_place(l)
                        keys, queries = (g_qk[:, l, :], g_qk[:, l, :]) if l < 8 else (mix[:, 28 + h, :], mix[:, 24 + h, :])
                        if l == 0:
                            ins = M(PS[:, ps, 0:P], keys[:, 0:P], queries[:, P:2 * P], start=True, stop=True)
                            continue
                        for t in range(2):
                            ins = M(PS[:, ps + bank, c0 + t * P:c0 + (t + 1) * P], keys[:, t * P:(t + 1) * P],
                                    queries[:, t * P:(t + 1) * P], start=True, stop=True)
                    ins.then_inc(S["g_score"], 1)
                if n in GLA_TURN and j == 2:
                    turn_values(GLA_TURN[n], ps + 2)
                if n in GLA_HEAD and j == 5:
                    h = GLA_HEAD[n]
                    values = turned_values(32 + NB * (h // 2))
                    wait("g_merged", 9)
                    for v in range(2):
                        c0 = (h % 2) * GDV + v * P
                        ins = causal_sum(PS[:, ps + 1, v * T:(v + 1) * T], values[:, 0, c0:c0 + P], values[:, 1, c0:c0 + P], g_sc)
                    ins.then_inc(S["g_out"], 1)
                if n in GLA_NORM and j == 1:
                    wait("g_sq")
                    for v in range(2):
                        ins = M(PS[:, ps + 3, 0:T], ones[:, :], g_sq[:, v, :], start=(v == 0), stop=(v == 1))
                    ins.then_inc(S["g_ss"], 1)
                if j == layers["in2"].G - 1:
                    if n == 1:
                        wait("g_pre", GH)
                    if n in GLA_HEAD:
                        wait("g_o")
                    if n in GLA_NORM:
                        pe.wait_ge(S["g_var"], GLA_NORM[n] + 1)

            stream("in2", blocks_of(xs), ready=17, chunks=NORM_CHUNKS, side=mixers2)
            stream("out2", lambda c: cf[c // NB][:, c % NB, :] if c < 2 * NB else xs[:, c, :], ready=22, side=sums_beside("out2"))
            strip_sum(spare("out2", 3) + 3)
            sum_squares(mix[:, 40:56, :], 0, KC, PS[:, 0, 0:T])

            stream("up2", blocks_of(xs), ready=26, chunks=NORM_CHUNKS)
            stream("down2", blocks_of(hs), side=down_side("down2", "up2"))
            strip_sum(spare("down2", 3) + 3)

            all_out("down2")
            for k in range(4):
                wait("res_made")
                for t in range(2):
                    for b in range(NB):
                        ins = nc.tensor.transpose(PS[:, 2 * k + t, b * P:(b + 1) * P], xT[:, NB * k + b, t * P:(t + 1) * P],
                                                  ident[:, :])
                ins.then_inc(S["y_turned"], 1)


_INS = ["x", "p", "mix_norm_g", "w_in", "mlstm_gate_bias", "mlstm_out_g", "fox_q_g", "fox_k_g", "fox_f_bias", "w_out",
        "ffn_norm_g", "w_up", "conv_w", "conv_b", "w_down", "ple_norm_g", "w_ple_gate", "w_ple_proj", "c_2", "w_mod_2",
        "b_mod_2", "mix_pre_w_2", "mix_post_w_2", "w_in_2", "conv_w_2", "gate_w2_2", "gate_b_2", "gla_norm_w_2",
        "w_out_2", "ffn_pre_w_2", "ffn_post_w_2", "w_up_2", "ffn_conv_w_2", "w_down_2"]


def kernel(**inputs):
    import numpy as np
    import concourse.bacc as bacc
    from concourse.bass_utils import run_bass_kernel_spmd

    nc = bacc.Bacc("TRN2", target_bir_lowering=False, num_devices=1)
    arrays, aps = {}, {}
    for name in _INS:
        array = np.ascontiguousarray(inputs[name])
        arrays[f"in_{name}"] = array
        aps[name] = nc.dram_tensor(f"in_{name}", array.shape, mybir.dt.from_np(array.dtype), kind="ExternalInput").ap()
    out = nc.dram_tensor("out", (1, T, D), F32, kind="ExternalOutput").ap()
    two_block_kernel(nc, aps, out)
    result = run_bass_kernel_spmd(nc, [arrays], core_ids=[0])
    return result.results[0]["out"]
```
